# Optimizing a Trainium2 kernel written in Bass

```python
import math
import jax, jax.numpy as jnp
from jax import lax
import numpy as np

D_MODEL = 1024
BATCH = 1
SEQ = 128
DEPTH = 1
DEC_BATCH = 1
DEC_SEQ = 1024
PAST_LEN = 128

GRID_W = 64
D_MIX = D_MODEL
D_POOL = D_MIX // 2
POOL_WINDOWS = (2, 4, 8, 16)
POOL_GROUP = D_POOL // len(POOL_WINDOWS)
D_SSM = D_MIX - D_POOL
SSM_P = 16
SSM_G = D_SSM // SSM_P
SSM_N = 64
D_FF = 4 * D_MODEL
EPS = 1e-6

kernel_name = "hybrid_pool_s5_dit_prefix_step"

F32 = jnp.float32

def _rmsnorm(x, g):
    xf = x.astype(F32)
    y = xf * lax.rsqrt(jnp.mean(xf * xf, axis=-1, keepdims=True) + EPS) * g.astype(F32)
    return y.astype(x.dtype)

def _adaln(cvec, w, b):
    m = jnp.dot(jax.nn.silu(cvec), w) + b
    return [t[:, None, :] for t in jnp.split(m, 6, axis=-1)]

def _bounds(n, w):
    t = jnp.arange(n)
    return jnp.clip(t - w // 2, 0, n), jnp.clip(t + w // 2, 0, n)

def _pool_mean_1d(u, w):
    n = u.shape[1]
    s = jnp.pad(jnp.cumsum(u, axis=1), ((0, 0), (1, 0), (0, 0)))
    lo, hi = _bounds(n, w)
    tot = jnp.take(s, hi, axis=1) - jnp.take(s, lo, axis=1)
    cnt = (hi - lo).astype(F32)[None, :, None]
    return tot / cnt

def _pool_mean_2d(u, w, rows):
    b, n, ch = u.shape
    g = u.reshape(b, rows, GRID_W, ch)
    s = jnp.cumsum(jnp.cumsum(g, axis=1), axis=2)
    s = jnp.pad(s, ((0, 0), (1, 0), (1, 0), (0, 0)))
    r0, r1 = _bounds(rows, w)
    c0, c1 = _bounds(GRID_W, w)

    def corner(r, c):
        return jnp.take(jnp.take(s, r, axis=1), c, axis=2)

    tot = corner(r1, c1) - corner(r0, c1) - corner(r1, c0) + corner(r0, c0)
    cnt = ((r1 - r0)[:, None] * (c1 - c0)[None, :]).astype(F32)[None, :, :, None]
    return (tot / cnt).reshape(b, n, ch)

def _pool_mixer(u, pool_w, pool_scale, rows):
    outs = []
    for gi, w in enumerate(POOL_WINDOWS):
        ug = u[..., gi * POOL_GROUP:(gi + 1) * POOL_GROUP].astype(F32)
        pm = _pool_mean_1d(ug, w) if rows is None else _pool_mean_2d(ug, w, rows)
        outs.append(jnp.einsum("blc,cd->bld", pm - ug, pool_w[gi].astype(F32)))
    out = jnp.concatenate(outs, axis=-1) * pool_scale.astype(F32)
    return out.astype(u.dtype)

def _discretize(a_re, a_im, log_dt, b_re, b_im):
    a = lax.complex(a_re.astype(F32), a_im.astype(F32))
    dt = jnp.exp(log_dt.astype(F32))[:, None]
    a_bar = jnp.exp(a * dt)
    bmat = lax.complex(b_re.astype(F32), b_im.astype(F32))
    b_bar = ((a_bar - 1.0) / a)[..., None] * bmat
    return a_bar, b_bar

def _combine(e1, e2):
    a1, b1 = e1
    a2, b2 = e2
    return a1 * a2, a2 * b1 + b2

def _ssm_mixer(u, p, h0):
    bsz, n, _ = u.shape
    ug = u.astype(F32).reshape(bsz, n, SSM_G, SSM_P)
    uc = ug.astype(jnp.complex64)
    y = p["ssm_d"].astype(F32) * ug
    finals = []
    for d in range(2):
        rev = d == 1
        a_bar, b_bar = _discretize(p["ssm_a_re"][d], p["ssm_a_im"][d], p["ssm_log_dt"][d],
                                   p["ssm_b_re"][d], p["ssm_b_im"][d])
        bu = jnp.einsum("gnp,blgp->blgn", b_bar, uc)
        if h0 is not None:
            bu = bu.at[:, -1 if rev else 0].add(a_bar * h0[d])
        _, h = lax.associative_scan(_combine, (jnp.broadcast_to(a_bar, bu.shape), bu),
                                    reverse=rev, axis=1)
        cmat = lax.complex(p["ssm_c_re"][d].astype(F32), p["ssm_c_im"][d].astype(F32))
        y = y + jnp.real(jnp.einsum("gpn,blgn->blgp", cmat, h))
        finals.append(h[:, 0] if rev else h[:, -1])
    y = jax.nn.gelu(y.reshape(bsz, n, D_SSM))
    out = y * jax.nn.sigmoid(jnp.dot(y, p["ssm_w_glu"].astype(F32)))
    return out.astype(u.dtype), finals

def _layer(x, cvec, p, rows, h0):
    sh1, sc1, g1, sh2, sc2, g2 = _adaln(cvec, p["w_ada"], p["b_ada"])
    h = _rmsnorm(x, p["norm_mix"]) * (1 + sc1) + sh1
    proj = jnp.dot(h, p["w_in"])
    pool_out = _pool_mixer(proj[..., :D_POOL], p["pool_w"], p["pool_scale"], rows)
    ssm_out, finals = _ssm_mixer(proj[..., D_POOL:], p, h0)
    mix = jnp.dot(jnp.concatenate([pool_out, ssm_out], axis=-1), p["w_out"])
    x = x + g1 * mix.astype(x.dtype)
    h = _rmsnorm(x, p["norm_mlp"]) * (1 + sc2) + sh2
    f = jnp.square(jax.nn.relu(jnp.dot(h, p["w_mlp1"])))
    x = x + g2 * jnp.dot(f, p["w_mlp2"]).astype(x.dtype)
    return x, finals

def setup_inputs(seed: int = 0) -> dict:
    key = jax.random.key(seed)
    ks = iter(jax.random.split(key, 40))

    def nrm(shape, scale):
        return jax.random.normal(next(ks), shape, F32) * scale

    n_idx = jnp.arange(SSM_N, dtype=F32)
    return {
        "x_prompt": nrm((BATCH, SEQ, D_MODEL), 1.0),
        "x_sample": nrm((DEC_BATCH, DEC_SEQ, D_MODEL), 1.0),
        "state_ssm": nrm((DEC_BATCH, DEPTH, 2, SSM_G, SSM_N, 2), 0.3),
        "c": nrm((DEC_BATCH, D_MODEL), 1.0),
        "c_ctx": nrm((D_MODEL,), 1.0),
        "norm_mix": 1.0 + nrm((DEPTH, D_MODEL), 0.02),
        "norm_mlp": 1.0 + nrm((DEPTH, D_MODEL), 0.02),
        "w_ada": nrm((DEPTH, D_MODEL, 6 * D_MODEL), 0.5 * D_MODEL ** -0.5),
        "b_ada": nrm((DEPTH, 6 * D_MODEL), 0.02),
        "w_in": nrm((DEPTH, D_MODEL, D_MIX), D_MODEL ** -0.5),
        "w_out": nrm((DEPTH, D_MIX, D_MODEL), D_MIX ** -0.5),
        "pool_w": nrm((DEPTH, len(POOL_WINDOWS), POOL_GROUP, POOL_GROUP), POOL_GROUP ** -0.5),
        "pool_scale": 1.0 + nrm((DEPTH, D_POOL), 0.1),
        "ssm_a_re": -0.5 + nrm((DEPTH, 2, SSM_G, SSM_N), 0.01),
        "ssm_a_im": math.pi * n_idx + nrm((DEPTH, 2, SSM_G, SSM_N), 0.01),
        "ssm_log_dt": jax.random.uniform(next(ks), (DEPTH, 2, SSM_G), F32,
                                         math.log(1e-3), math.log(1e-1)),
        "ssm_b_re": nrm((DEPTH, 2, SSM_G, SSM_N, SSM_P), (0.5 / SSM_P) ** 0.5),
        "ssm_b_im": nrm((DEPTH, 2, SSM_G, SSM_N, SSM_P), (0.5 / SSM_P) ** 0.5),
        "ssm_c_re": nrm((DEPTH, 2, SSM_G, SSM_P, SSM_N), (0.5 / SSM_N) ** 0.5),
        "ssm_c_im": nrm((DEPTH, 2, SSM_G, SSM_P, SSM_N), (0.5 / SSM_N) ** 0.5),
        "ssm_d": nrm((DEPTH, SSM_G, SSM_P), 1.0),
        "ssm_w_glu": nrm((DEPTH, D_SSM, D_SSM), D_SSM ** -0.5),
        "w_mlp1": nrm((DEPTH, D_MODEL, D_FF), D_MODEL ** -0.5),
        "w_mlp2": nrm((DEPTH, D_FF, D_MODEL), D_FF ** -0.5),
        "norm_out": 1.0 + nrm((D_MODEL,), 0.02),
    }

def reference(x_prompt, x_sample, state_ssm, c, c_ctx, norm_mix, norm_mlp, w_ada, b_ada,
              w_in, w_out, pool_w, pool_scale, ssm_a_re, ssm_a_im, ssm_log_dt, ssm_b_re,
              ssm_b_im, ssm_c_re, ssm_c_im, ssm_d, ssm_w_glu, w_mlp1, w_mlp2, norm_out):
    rows = x_sample.shape[1] // GRID_W

    def layer_params(l):
        return dict(norm_mix=norm_mix[l], norm_mlp=norm_mlp[l], w_ada=w_ada[l], b_ada=b_ada[l],
                    w_in=w_in[l], w_out=w_out[l], pool_w=pool_w[l], pool_scale=pool_scale[l],
                    ssm_a_re=ssm_a_re[l], ssm_a_im=ssm_a_im[l], ssm_log_dt=ssm_log_dt[l],
                    ssm_b_re=ssm_b_re[l], ssm_b_im=ssm_b_im[l], ssm_c_re=ssm_c_re[l],
                    ssm_c_im=ssm_c_im[l], ssm_d=ssm_d[l], ssm_w_glu=ssm_w_glu[l],
                    w_mlp1=w_mlp1[l], w_mlp2=w_mlp2[l])

    xp = x_prompt
    cctx = c_ctx[None, :]
    ctx_states = []
    for l in range(DEPTH):
        xp, finals = _layer(xp, cctx, layer_params(l), None, None)
        hs = jnp.stack(finals, axis=1)
        ctx_states.append(jnp.stack([jnp.real(hs), jnp.imag(hs)], axis=-1))
    new_state_ssm = jnp.stack(ctx_states, axis=1)
    y_prompt = _rmsnorm(xp, norm_out)

    xs = x_sample
    st = state_ssm.astype(F32)
    for l in range(DEPTH):
        h0 = lax.complex(st[:, l, ..., 0], st[:, l, ..., 1])
        xs, _ = _layer(xs, c, layer_params(l), rows, (h0[:, 0], h0[:, 1]))
    y_sample = _rmsnorm(xs, norm_out)

    return (y_prompt, y_sample, new_state_ssm)


_drawn_inputs = setup_inputs


def setup_inputs(seed=0):
    import zlib

    import numpy as np

    out = dict(_drawn_inputs(seed))
    spreads = {}
    factors = {'state_ssm': 4.738,
     'norm_mix': 3.119,
     'norm_mlp': 6.582,
     'pool_scale': 2.874,
     'ssm_a_re': 4.353,
     'ssm_c_re': 5.579,
     'ssm_c_im': 5.411,
     'norm_out': 2.856}
    for name, (base, spread) in spreads.items():
        noise = np.random.default_rng([zlib.crc32(name.encode()), seed]).standard_normal(out[name].shape)
        drawn = base * np.exp(spread * noise) if base else spread * noise
        out[name] = __import__('jax').numpy.asarray(drawn.astype(out[name].dtype))
    for name, factor in factors.items():
        out[name] = (out[name] * factor).astype(out[name].dtype)
    return out
```

```python
import concourse.bass as bass
from concourse import mybir

F32 = mybir.dt.float32
F32R = mybir.dt.float32r
ALU = mybir.AluOpType
ACT = mybir.ActivationFunctionType

P = 128
D = 1024
KB = D // P
LAT, CTX = 1024, 128
T = LAT + CTX
TT = T // P
TG = 384
NG = T // TG
L = 8
CL, CC = LAT // L, CTX // L
CH = CL + CC
G, N, SP = 32, 64, 16
Q = 2 * G
DFF = 4 * D
FC = 256
NFC = DFF // FC
ROWS, GW = 16, 64
EPS = 1e-6
MAGIC = 1.5 * 2.0 ** 23
TWO_PI = (6.28125, 1.93500518798828125e-3, 3.0199159819e-7)
PITCH = GW + 8
PADDED = 31 * PITCH + 8
CPAD = CTX + 16

KBYTE = 1024
RESERVED = 16 * KBYTE + 128


def build(nc, x_prompt, x_sample, state_ssm, c, c_ctx, norm_mix, norm_mlp, w_ada, b_ada, w_in, w_out, pool_w,
          pool_scale, ssm_a_re, ssm_a_im, ssm_log_dt, ssm_b_re, ssm_b_im, ssm_c_re, ssm_c_im, ssm_d,
          ssm_w_glu, w_mlp1, w_mlp2, norm_out, inv_count, y_prompt, y_sample, new_state):
    V, S, PE, GP = nc.vector, nc.scalar, nc.tensor, nc.gpsimd

    def at(name, shape, offset, dt=F32):
        return nc.alloc_sbuf_tensor_at(name, list(shape), dt, offset=offset)

    R_X, R_W, R_RAW, R_A, R_U, R_P, R_S, R_C = (RESERVED + k * 512 for k in (0, 144, 208, 240, 304, 340, 376, 395))
    XH = at("x_hi", [P, KB, T], R_X, F32R)
    XL = at("x_lo", [P, KB, T], R_X + 36 * KBYTE, F32R)
    WH = [at(f"w_hi{i}", [P, 1024], R_W + i * 8 * KBYTE, F32R) for i in range(4)]
    WL = [at(f"w_lo{i}", [P, 1024], R_W + i * 8 * KBYTE + 4 * KBYTE, F32R) for i in range(4)]
    RAW = [at(f"raw{i}", [P, 1024], R_RAW + i * 4 * KBYTE) for i in range(4)]
    XS = [at(f"x_tile{i}", [P, D], R_W + 16 * KBYTE + i * 4 * KBYTE) for i in range(2)]
    B2 = at("b_bar_turned", [P, Q, SP], R_W + 24 * KBYTE)
    WB = at("to_state", [P, Q, P], R_A)
    SQ0 = at("square_dump0", [P, D], R_A)
    HT0 = [at(f"h_tile{i}", [P, KB, P], R_S + i * 4 * KBYTE) for i in range(2)]
    PROJ = [at(f"proj{i}", [P, T], R_S + i * 4608) for i in range(2)]
    POOL = at("pool_in", [P, 4, T], R_P)
    U = at("u_chunks", [P, G, CH], R_U)
    BX = at("b_re_im", [P, Q, SP], R_P)
    BY = at("b_im_re", [P, Q, SP], R_P + 4 * KBYTE)
    ROW0 = at("ada_row0", [2, 512], R_P + 8 * KBYTE)
    BIAS0 = at("ada_bias0", [1, 2048], R_P + 10 * KBYTE)
    small = [R_U]

    def tiny(name, shape):
        n = 4
        for x in shape[1:]:
            n *= x
        small[0] += (n + 31) // 32 * 32
        return at(name, shape, small[0] - (n + 31) // 32 * 32)

    VEC = tiny("vector_rows", [36, P])
    LDT = tiny("log_dt", [Q, 1])
    DT = tiny("dt", [Q, 1])
    AR, AI, EX, TH, KT, RT = (tiny(n, [Q, N]) for n in ("a_re", "a_im", "growth", "angle", "turns", "rest"))
    SR, SH, C0, NR, DEN, RD = (tiny(n, [Q, N]) for n in ("sine", "half_sine", "cosine", "nom", "den", "rden"))
    M1, M2, M3, M4 = (tiny(f"m{i}", [Q, N]) for i in range(4))
    TAB = tiny("tables", [Q, 4, P])
    ZR, ZS, ZT, ZU = (tiny(n, [P, Q]) for n in ("z_re", "z_im_signed", "z_re_signed", "z_im_neg"))
    ZI = tiny("z_im", [P, Q])
    SGN = tiny("sign", [P, 1])
    TB = tiny("b_tmp", [P, Q, SP])
    TW = [tiny(f"to_state_tmp{i}", [P, G, SP]) for i in range(2)]
    PT = [tiny(f"pow_tmp{i}", [P, 4, Q]) for i in range(2)]
    assert small[0] <= R_P
    B1 = at("b_bar", [P, Q, SP], R_C)
    PR = at("pow_re", [P, L + 1, Q], R_C + 4096)
    PI = at("pow_im", [P, L + 1, Q], R_C + 6400)
    ID = at("identity", [P, P], R_C + 8704)
    AQ = at("a8_im_signed", [P, Q], R_C + 9216)
    FIN = at("ctx_final", [P, Q], R_C + 9472)
    ADA = [at(f"ada_cols{i}", [P, 2, KB], R_C + 9728 + 64 * i) for i in range(4)]
    COL = at("vector_cols", [P, 36], R_C + 9984)
    EPSB = at("eps", [P, 1], R_C + 10144)
    CSG = at("c_sign", [P, 1], R_C + 10176)
    ONE = at("ones", [1, 2], R_C + 10208)
    STAT = [at(f"stat{i}", [P, TT], R_S + 8192 + 64 * i) for i in range(3)]
    H = at("states", [P, 2, G, CH], R_X)
    CA = at("from_state", [P, Q, P], R_X + 36 * KBYTE)
    ROW2 = at("ada_row2", [2, 512], R_X + 68 * KBYTE)
    BIAS2 = at("ada_bias2", [1, 512], R_X + 70 * KBYTE)
    C1 = at("c_signed", [P, Q, SP], R_W)
    C2 = at("c_turned", [P, Q, SP], R_W + 4 * KBYTE)
    PAD = [at(f"padded{i}", [P, PADDED + CPAD], R_W + 8 * KBYTE + i * 9536) for i in range(2)]
    LOC = at("local", [P, G, P], R_W + 8 * KBYTE)
    o = R_W + 8 * KBYTE + 2 * 9536
    PS_, QS_, RS_ = (at(f"step_{n}", [P, 2, Q], o + 512 * k) for k, n in enumerate("pqr"))
    DD = at("d_diag", [SP, G, SP], o + 1536)
    ST = at("state_rows", [Q, N, 2], o + 1536 + 2048)
    STR = at("state_rows_split", [Q, 2, N], o + 1536 + 2560)
    KK = at("kernels", [SP, G, 15, SP], R_A)
    CT = at("ca_tmp", [P, G, SP], R_A + 30 * KBYTE)
    EST = [at(f"pooled{i}", [P, TG], R_S + i * 1536) for i in range(2)]
    CS = at("c_rows", [P, 8, 3, N], R_X + 36 * KBYTE)
    PWS = at("pool_w_sb", [P, 4, P], R_S + 3072)
    INV = at("inv_count_b", [P, T], R_S + 5120)
    Y = at("y_chunks", [P, G, CH], R_P)
    ACC = at("acc", [P, TT, D], R_A)
    o3 = R_A + 36 * KBYTE
    YR = at("y_rows", [P, 4, T], o3)
    YH = at("y_hi", [P, 4, TG], o3 + 18 * KBYTE, F32R)
    YL = at("y_lo", [P, 4, TG], o3 + 24 * KBYTE, F32R)
    MP = at("pooled_rows", [P, 4, TG], o3 + 30 * KBYTE)
    SZ = [at(f"sigmoid{i}", [P, TG], o3 + 36 * KBYTE + 1536 * i) for i in range(2)]
    SO = at("ssm_out", [P, TG], o3 + 39 * KBYTE)
    GB = at("gate_b", [P, 2, D], R_C)
    FH = at("f_hi", [P, 2, T], o3, F32R)
    FL = at("f_lo", [P, 2, T], o3 + 9 * KBYTE, F32R)
    RL = [at(f"relu{i}", [P, TG], o3 + 18 * KBYTE + 1536 * i) for i in range(2)]
    FT = [at(f"f_tmp{i}", [P, TG], o3 + 21 * KBYTE + 1536 * i) for i in range(2)]
    BT = [at(f"gated{i}", [P, 512], o3 + 24 * KBYTE + 2048 * i) for i in range(4)]
    HT1 = [at(f"h1_tile{i}", [P, KB, P], o3 + 24 * KBYTE + i * 4 * KBYTE) for i in range(2)]
    XN = [at(f"xn_tile{i}", [P, D], o3 + 32 * KBYTE + i * 4 * KBYTE) for i in range(2)]
    NO = at("norm_out_b", [P, D], o3 + 32 * KBYTE)
    SQ = at("square_dump", [P, D], o3 + 36 * KBYTE)
    SQ1 = at("square_dump1", [P, D], o3 + 8 * KBYTE)
    BT3 = [at(f"gated3_{i}", [P, 512], o3 + 2048 * i) for i in range(4)]

    BANK = [nc.alloc_psum_tensor(f"bank{i}", [P, 512], F32) for i in range(8)]

    def scratch(name, shape):
        return nc.dram_tensor(name, shape, F32, kind="Internal").ap()

    UD, YD, MD = scratch("u_rows", (512, T)), scratch("ssm_rows", (512, T)), scratch("pool_rows", (512, T))
    GD = scratch("gates", (2, 2, D))

    names = ["raw0", "raw1", "raw2", "raw3", "ada_used", "w_hi", "w_split", "mm_act", "mm_dve", "ev_act",
             "ev_dve", "vec_in", "dtab_in", "b_in", "bias0_in", "xt0", "xt1", "id_ready", "id_zero", "sgn_ready",
             "dve", "pe_small", "col_ready", "silu_done", "ada_mm", "row_ready", "ada_cols",
             "tab_dt", "tab_e", "tab_th", "tab_sin", "wbt", "wbt_mm", "wb_ready", "sq", "root", "xn", "tr", "aff_d", "aff_a",
             "h_hi", "h_lo", "ud_w0", "ud_w1", "ud_w2", "ud_w3", "u_in0", "u_in1", "st_in",
             "cs_in", "inv_in", "dd_in", "dd_ready", "c_mm", "c_ready", "h0_mm", "h_init", "pad_zero", "pooled",
             "ca", "ca_ready", "sc_p", "sc_r", "sc_h", "cx_r", "cx_h", "gates_w", "bias2_in", "pw_in",
             "md_w0", "md_w1", "kk_mm", "kk_ready", "loc_in", "yd_w", "yr0", "yr1", "yr2", "mp_in",
             "y_split_hi", "y_split", "so", "mix_hi", "mix_pool", "mix_ready", "gb_in",
             "acc_in", "acc", "gp", "f_ready", "fin_mm", "fin_ready", "fin_out", "no_in", "y_final",
             "out_w", "acts", "tabs", "ada0", "sqr"]
    sem = {n: nc.alloc_semaphore(n) for n in names}
    s = type("Sems", (), sem)

    N_ADA0, N_IN, N_ADA2, N_GLU, N_OUT = 16, 8, 32, 2, 8
    FIRST_IN = N_ADA0
    FIRST_ADA2 = FIRST_IN + N_IN
    FIRST_GLU = FIRST_ADA2 + N_ADA2
    FIRST_OUT = FIRST_GLU + N_GLU
    FIRST_MLP = FIRST_OUT + N_OUT
    raw_in = [s.raw0, s.raw1, s.raw2, s.raw3]
    PARTS = [1, 0, 2, 3, 4, 5]

    def raw_landed(eng, n):
        eng.wait_ge(raw_in[n % 4], 16 * (n // 4 + 1))

    def w_slot(w):
        return w % 2 if w < N_IN else (w - N_IN) % 4

    ada_v = w_ada[0].rearrange("(k p) n -> p k n", p=P)
    in_v = w_in[0].rearrange("(k p) n -> p k n", p=P)
    glu_v = ssm_w_glu[0].rearrange("(k p) n -> p k n", p=P)
    w1_v = w_mlp1[0].rearrange("(k p) n -> p k n", p=P)
    xs_v = x_sample[0].rearrange("(c j) d -> c j d", j=L)
    xp_v = x_prompt[0].rearrange("(c j) d -> j c d", j=L)
    ys_v = y_sample[0].rearrange("(c j) d -> c j d", j=L)
    yp_v = y_prompt[0].rearrange("(c j) d -> j c d", j=L)

    A_STRAIGHT = 96
    B_STRAIGHT = 72
    def turn_banks(t, odd):
        return (BANK[4], BANK[5]) if t % 2 == 0 else (BANK[odd], BANK[odd + 1])

    LAG = 3
    DVE_WINDOWS = 3

    def grid(buf, r0, r1, shift=0):
        o = (r0 + 8) * PITCH + 8
        return buf[:, o:o + (r1 - r0) * PITCH].rearrange("p (r c) -> p r c", c=PITCH)[:, :, shift:shift + GW]

    def ctx(buf, lo, hi):
        return buf[:, PADDED + 8 + lo:PADDED + 8 + hi]

    def pool_window(eng, tt, then, copy, gi):
        w = 2 << gi
        eng.wait_ge(s.pad_zero, 2 * gi + 2)
        a_, b_ = PAD
        lat_in = POOL[:, gi, 0:LAT].rearrange("p (r c) -> p r c", c=GW)
        then(copy(grid(a_, 0, ROWS), lat_in))
        then(copy(ctx(a_, 0, CTX), POOL[:, gi, LAT:T]))
        first, last = 8 * PITCH + 8, (8 + ROWS - 1) * PITCH + 8 + GW
        for st in range(gi + 1):
            back, ahead = (1, 0) if st == 0 else (1 << (st - 1), 1 << (st - 1))
            ext = w // 2 - (1 << st)
            lo, hi = first - ext, last + ext
            then(tt(b_[:, lo:hi], a_[:, lo - back:hi - back], a_[:, lo + ahead:hi + ahead], ALU.add))
            then(tt(ctx(b_, -ext, CTX + ext), ctx(a_, -ext - back, CTX + ext - back),
                    ctx(a_, -ext + ahead, CTX + ext + ahead), ALU.add))
            a_, b_ = b_, a_
        sums = a_
        for st in range(gi + 1):
            back, ahead = (1, 0) if st == 0 else (1 << (st - 1), 1 << (st - 1))
            ext = w // 2 - (1 << st)
            then(tt(grid(b_, -ext, ROWS + ext), grid(a_, -ext - back, ROWS + ext - back),
                    grid(a_, -ext + ahead, ROWS + ext + ahead), ALU.add))
            a_, b_ = b_, a_
        eng.wait_ge(s.inv_in, 16 * (gi + 1))
        then(tt(grid(a_, 0, ROWS), grid(a_, 0, ROWS), INV[:, 0:LAT].rearrange("p (r c) -> p r c", c=GW), ALU.mult))
        then(tt(ctx(sums, 0, CTX), ctx(sums, 0, CTX), INV[:, LAT:T], ALU.mult))
        then(tt(lat_in, grid(a_, 0, ROWS), lat_in, ALU.subtract))
        tt(POOL[:, gi, LAT:T], ctx(sums, 0, CTX), POOL[:, gi, LAT:T], ALU.subtract).then_inc(s.pooled, 1)
        eng.wait_ge(s.pooled, gi + 1)

    block = nc.Block()
    block.__enter__()

    def lat_j3(ap):
        return ap.rearrange("p (j c) -> p j c", c=CL)

    uds = [s.ud_w0, s.ud_w1, s.ud_w2, s.ud_w3]

    @block.sync
    def _(sp):
        def free(n):
            m = n - 4
            if m < 0:
                return
            if m < FIRST_IN:
                sp.wait_ge(s.ada_used, m + 1)
            elif m < FIRST_ADA2:
                sp.wait_ge(s.w_split, m - FIRST_IN + 1)
            elif m < FIRST_GLU:
                sp.wait_ge(s.ada_used, N_ADA0 + m - FIRST_ADA2 + 1)
            else:
                sp.wait_ge(s.w_split, N_IN + m - FIRST_GLU + 1)

        def load(n, dst, src):
            free(n)
            sp.dma_start(dst, src).then_inc(raw_in[n % 4], 16)

        def load_ada(n, i):
            part, k = PARTS[i // KB], i % KB
            load(n, RAW[n % 4][:], ada_v[:, k, part * D:(part + 1) * D])

        for i in range(N_ADA0):
            load_ada(i, i)
        for i in range(N_IN):
            n = FIRST_IN + i
            load(n, RAW[n % 4][:].rearrange("p (k f) -> p k f", k=KB), in_v[:, :, i * P:(i + 1) * P])
        for i in range(4):
            load_ada(FIRST_ADA2 + i, N_ADA0 + i)
        sp.wait_ge(s.wbt, 2 * L)
        for half in range(2):
            sp.wait_ge(uds[2 * half], 16)
            sp.wait_ge(uds[2 * half + 1], 16)
            g0 = 16 * half
            ud = UD[g0 * SP:(g0 + 16) * SP, :].rearrange("(g p) t -> p g t", p=SP)
            for j in range(L):
                dst = U[j * SP:(j + 1) * SP, g0:g0 + 16, :]
                sp.dma_start(dst[:, :, 0:CL], ud[:, :, j * CL:(j + 1) * CL]).then_inc(s.u_in0 if half == 0 else s.u_in1, 16)
                sp.dma_start(dst[:, :, CL:CH], ud[:, :, LAT + j * CC:LAT + (j + 1) * CC])\
                  .then_inc(s.u_in0 if half == 0 else s.u_in1, 16)
        sp.wait_ge(s.mm_act, 24)
        sp.dma_start(ST[:].rearrange("q n r -> q (n r)"), state_ssm[0, 0].rearrange("d g n r -> (d g) (n r)")).then_inc(s.st_in, 16)
        for k, src in enumerate((ssm_c_re, ssm_c_im, ssm_c_re)):
            sp.dma_start(CS[:, :, k, :], src[0].rearrange("d (b g) p n -> (g p) (d b) n", g=8)).then_inc(s.cs_in, 16)
        sp.dma_start(DD[:].rearrange("p g c -> p (g c)"), ssm_d[0].rearrange("g p -> (g p)").partition_broadcast(SP)).then_inc(s.dd_in, 16)
        for i in range(4, N_ADA2):
            load_ada(FIRST_ADA2 + i, N_ADA0 + i)
        for i in range(N_GLU):
            n = FIRST_GLU + i
            load(n, RAW[n % 4][:].rearrange("p (k f) -> p k f", k=2), glu_v[:, 2 * i:2 * i + 2, :])
        for i in range(2):
            n = FIRST_OUT + i
            load(n, RAW[n % 4][:], w_out[0, i * P:(i + 1) * P, :])
        sp.wait_ge(s.ev_act, 84)
        yd = YD.rearrange("(g p) t -> p g t", p=SP)
        for j in range(L):
            src = Y[j * SP:(j + 1) * SP, :, :]
            sp.dma_start(yd[:, :, j * CL:(j + 1) * CL], src[:, :, 0:CL]).then_inc(s.yd_w, 16)
            sp.dma_start(yd[:, :, LAT + j * CC:LAT + (j + 1) * CC], src[:, :, CL:CH]).then_inc(s.yd_w, 16)
        sp.wait_ge(s.yd_w, 16 * 16)
        yds = YD.rearrange("(k p) t -> p k t", p=P)
        for g, q in enumerate((s.yr0, s.yr1, s.yr2)):
            sp.dma_start(YR[:, :, g * TG:(g + 1) * TG], yds[:, :, g * TG:(g + 1) * TG]).then_inc(q, 16)
        sp.wait_ge(s.fin_ready, 1)
        sp.dma_start(new_state[0, 0].rearrange("d g n r -> (d g) (n r)"), ST[:].rearrange("q n r -> q (n r)")).then_inc(s.fin_out, 16)
        sp.wait_ge(s.md_w0, 16 * 6)
        sp.wait_ge(s.md_w1, 16 * 6)
        mds = MD.rearrange("(k p) t -> p k t", p=P)
        for g in range(NG):
            if g:
                sp.wait_ge(s.mix_pool, g)
            sp.dma_start(MP[:], mds[:, :, g * TG:(g + 1) * TG]).then_inc(s.mp_in, 16)
            if g == 0:
                sp.dma_start(ACC[:, 0:L, :], xs_v).then_inc(s.acc_in, 16)
                for j in range(L):
                    sp.dma_start(ACC[j * CC:(j + 1) * CC, L, :], xp_v[j]).then_inc(s.acc_in, 16)
        for i in range(2, N_OUT):
            n = FIRST_OUT + i
            load(n, RAW[n % 4][:], w_out[0, i * P:(i + 1) * P, :])
        with sp.Fori(0, NFC) as ch:
            for i in range(4):
                n = FIRST_MLP + i
                sp.wait_ge(s.w_split, ch * 4 + (N_IN + n - 4 - FIRST_GLU + 1))
                if i < 2:
                    dst, src = RAW[n % 4][:].rearrange("p (k f) -> p k f", k=4), w1_v[:, 4 * i:4 * i + 4, bass.ds(ch * FC, FC)]
                else:
                    dst, src = RAW[n % 4][:], w_mlp2[0, bass.ds(ch * FC + (i - 2) * P, P), :]
                sp.dma_start(dst, src).then_inc(raw_in[n % 4], 16)
        for t in range(TT):
            sp.wait_ge(s.y_final, t + 1)
            if t < L:
                sp.dma_start(ys_v[:, t, :], ACC[:, t, :]).then_inc(s.out_w, 16)
            else:
                for j in range(L):
                    sp.dma_start(yp_v[j], ACC[j * CC:(j + 1) * CC, t, :]).then_inc(s.out_w, 16)
        sp.wait_ge(s.out_w, 16 * (2 * L))
        sp.wait_ge(s.fin_out, 16)

    @block.gpsimd
    def _(gp):
        steps = [0]

        def gp_then(inst):
            steps[0] += 1
            inst.then_inc(s.gp, 1)
            gp.wait_ge(s.gp, steps[0])

        GP.memset(ID[:], 0.0).then_inc(s.id_zero, 1)
        gp.wait_ge(s.id_zero, 1)
        GP.affine_select(out=ID[:], in_=ID[:], compare_op=ALU.not_equal, fill=1.0, base=0, pattern=[[-1, P]],
                         channel_multiplier=1).then_inc(s.id_ready, 1)
        gp.wait_ge(s.id_ready, 1)
        GP.memset(SGN[0:N, :], -1.0).then_inc(s.sgn_ready, 1)
        gp.wait_ge(s.sgn_ready, 1)
        GP.memset(SGN[N:P, :], 1.0).then_inc(s.sgn_ready, 1)
        gp.wait_ge(s.sgn_ready, 2)
        GP.memset(ONE[:], 1.0).then_inc(s.sgn_ready, 1)
        for t in range(TT):
            if t >= 2:
                gp.wait_ge(s.tr, t - 1)
            q = s.xt0 if t % 2 == 0 else s.xt1
            if t < L:
                gp.dma_start(XS[t % 2][:], xs_v[:, t, :]).then_inc(q, 16)
            else:
                for j in range(L):
                    gp.dma_start(XS[t % 2][j * CC:(j + 1) * CC, :], xp_v[j]).then_inc(q, 16)
        def window_setup(gi):
            if gi:
                gp.wait_ge(s.pooled, gi)
            for i in range(2):
                GP.memset(PAD[i][:], 0.0).then_inc(s.pad_zero, 1)
                gp.wait_ge(s.pad_zero, 2 * gi + i + 1)
            if gi == 0:
                for q in uds:
                    gp.wait_ge(q, 16)
                gp.dma_start(PWS[:], pool_w[0].rearrange("i c d -> c i d")).then_inc(s.pw_in, 16)
            gp.dma_start(INV[:], inv_count[gi].partition_broadcast(P)).then_inc(s.inv_in, 16)

        gp.wait_ge(s.mm_act, 24)
        for gi in range(DVE_WINDOWS):
            window_setup(gi)
        gp.wait_ge(s.mm_act, 56)
        gp.wait_ge(s.c_ready, 16)
        n = 0
        for d in range(2):
            for j in range(L):
                e = j + 1 if d == 0 else L - j
                q0 = d * G
                out = CA[:, q0:q0 + G, j * SP:(j + 1) * SP]
                pr = PR[:, e, q0:q0 + G].unsqueeze(2).to_broadcast([P, G, SP])
                pi = PI[:, e, q0:q0 + G].unsqueeze(2).to_broadcast([P, G, SP])
                if n:
                    gp.wait_ge(s.ca_ready, n)
                GP.tensor_tensor(out, C1[:, q0:q0 + G, :], pr, ALU.mult).then_inc(s.ca, 1)
                gp.wait_ge(s.ca, 2 * n + 1)
                GP.tensor_tensor(CT[:], C2[:, q0:q0 + G, :], pi, ALU.mult).then_inc(s.ca, 1)
                n += 1
                gp.wait_ge(s.ca, 2 * n)
                GP.tensor_tensor(out, out, CT[:], ALU.add).then_inc(s.ca_ready, 1)
        gp.wait_ge(s.ca_ready, 2 * L)
        gp.wait_ge(s.dd_in, 16)
        GP.tensor_tensor(DD[:], DD[:], ID[0:SP, 0:SP].unsqueeze(1).to_broadcast([SP, G, SP]), ALU.mult).then_inc(s.dd_ready, 1)
        for gi in range(DVE_WINDOWS, 4):
            window_setup(gi)
            pool_window(gp, GP.tensor_tensor, gp_then, GP.tensor_copy, gi)
        gp.wait_ge(s.kk_ready, 16)
        gp.wait_ge(s.pooled, 4)
        kv = KK[:].rearrange("p g e c -> p g (e c)")
        for j in range(L):
            gp.dma_start(LOC[j * SP:(j + 1) * SP, :, :], kv[:, :, (L - 1 - j) * SP:(L - 1 - j) * SP + P]).then_inc(s.loc_in, 16)
        gp.wait_ge(s.gates_w, 16 * 2 * 2)
        gp.wait_ge(s.sc_h, CL - 1)
        gp.dma_start(GB[:].rearrange("p a d -> p (a d)"), GD[0].rearrange("a d -> (a d)").partition_broadcast(P)).then_inc(s.gb_in, 16)
        gp.wait_ge(s.acc_in, 16 * (L + 1))
        for i in range(B_STRAIGHT):
            o_ = i % 18
            gp.wait_ge(s.ev_dve, i + 1)
            a = ACC[:, o_ // 2, (o_ % 2) * 512:(o_ % 2) * 512 + 512]
            if i:
                gp.wait_ge(s.acc, i)
            GP.tensor_tensor(a, a, BT3[i % 4][:], ALU.add).then_inc(s.acc, 1)
        gp.wait_ge(s.ev_dve, B_STRAIGHT)
        gp.dma_start(GB[:].rearrange("p a d -> p (a d)"), GD[1].rearrange("a d -> (a d)").partition_broadcast(P)).then_inc(s.gb_in, 16)
        gp.wait_ge(s.tr, 2 * TT)
        gp.dma_start(NO[:], norm_out.partition_broadcast(P)).then_inc(s.no_in, 16)
        with gp.Fori(0, NFC) as ch:
            for i in range(18):
                gp.wait_ge(s.ev_dve, ch * 18 + (B_STRAIGHT + i + 1))
                gp.wait_ge(s.acc, ch * 18 + (B_STRAIGHT + i))
                a = ACC[:, i // 2, (i % 2) * 512:(i % 2) * 512 + 512]
                GP.tensor_tensor(a, a, BT[i % 4][:], ALU.add).then_inc(s.acc, 1)

    @block.scalar
    def _(act):
        for i, (v, n) in enumerate(((c[0], 8), (c_ctx, 8), (norm_mix[0], 8), (norm_mlp[0], 8), (pool_scale[0], 4))):
            act.dma_start(VEC[8 * i:8 * i + n, :], v.rearrange("(k p) -> k p", p=P)).then_inc(s.vec_in, 16)
        act.dma_start(LDT[:], ssm_log_dt[0].rearrange("d g -> (d g)").unsqueeze(1)).then_inc(s.dtab_in, 16)
        act.dma_start(AR[:], ssm_a_re[0].rearrange("d g n -> (d g) n")).then_inc(s.dtab_in, 16)
        act.dma_start(AI[:], ssm_a_im[0].rearrange("d g n -> (d g) n")).then_inc(s.dtab_in, 16)
        for k in range(2):
            part = PARTS[k]
            act.dma_start(BIAS0[:, k * D:(k + 1) * D], b_ada[:, part * D:(part + 1) * D]).then_inc(s.bias0_in, 16)
        for dst, top, bot in ((BX, ssm_b_re, ssm_b_im), (BY, ssm_b_im, ssm_b_re)):
            act.dma_start(dst[0:N], top[0].rearrange("d g n p -> n (d g) p")).then_inc(s.b_in, 16)
            act.dma_start(dst[N:P], bot[0].rearrange("d g n p -> n (d g) p")).then_inc(s.b_in, 16)
        act.wait_ge(s.dtab_in, 48)
        S.activation(DT[:], LDT[:], ACT.Exp).then_inc(s.tab_dt, 1)
        act.wait_ge(s.tab_th, 1)
        S.activation(EX[:], M1[:], ACT.Exp).then_inc(s.tab_e, 1)
        act.wait_ge(s.col_ready, 1)
        S.activation(COL[:, 0:16], COL[:, 0:16], ACT.Silu).then_inc(s.silu_done, 1)
        act.wait_ge(s.tab_th, 2)
        S.activation(SR[:], RT[:], ACT.Sin).then_inc(s.tab_sin, 1)
        S.activation(SH[:], RT[:], ACT.Sin, scale=0.5).then_inc(s.tab_sin, 1)

        def stats(t, src, dump, base):
            S.activation(dump, src, ACT.Square, accum_out=STAT[0][:, t:t + 1]).then_inc(s.sq, 1)
            act.wait_ge(s.sq, base + t + 1)
            S.activation(STAT[1][:, t:t + 1], STAT[0][:, t:t + 1], ACT.Sqrt, bias=EPSB[:], scale=1.0 / D).then_inc(s.root, 1)

        def affine(t, ht, ada, base):
            cond = 0 if t < L else 1
            act.wait_ge(s.tr, base + t + 1)
            if base + t >= 2:
                act.wait_ge(s.h_lo, base + t - 1)
            for k in range(4, KB):
                S.activation(ht[t % 2][:, k, :], turn_banks(t, 6 if base else 2)[1][:, (k - 4) * P:(k - 3) * P], ACT.Identity,
                             scale=ADA[ada][:, cond, k:k + 1], bias=ADA[ada + 1][:, cond, k:k + 1]).then_inc(s.aff_a, 1)

        def round_hi(t, ht, base):
            act.wait_ge(s.aff_a, 4 * (base + t + 1))
            act.wait_ge(s.aff_d, 4 * (base + t + 1))
            S.activation(XH[:, :, t * P:(t + 1) * P], ht[t % 2][:], ACT.Copy).then_inc(s.h_hi, 1)

        def split_hi(w, n):
            raw_landed(act, n)
            if w < N_IN:
                if w >= 2:
                    act.wait_ge(s.mm_act, 3 * (w - 1))
            elif w < N_IN + 4:
                act.wait_ge(s.mm_act, 84)
                if w == N_IN + 2:
                    act.wait_ge(s.fin_out, 16)
            elif w < N_IN + 6:
                act.wait_ge(s.mm_act, A_STRAIGHT)
            else:
                act.wait_ge(s.mm_dve, 18 * ((w - N_IN - 4) // 2))
            S.activation(WH[w_slot(w)][:], RAW[n % 4][:], ACT.Copy).then_inc(s.w_hi, 1)

        act.wait_ge(s.tabs, 2)
        for t in range(2):
            act.wait_ge(s.xt0 if t % 2 == 0 else s.xt1, 16)
            stats(t, XS[t % 2][:], HT0[t % 2][:].rearrange("p k c -> p (k c)"), 0)
        n_row = 0
        for part in range(2):
            for hf in range(2):
                act.wait_ge(s.ada_mm, part + 1)
                if n_row:
                    act.wait_ge(s.ada_cols, n_row)
                S.activation(ROW0[:], BANK[2 * part + hf][0:2, :], ACT.Copy).then_inc(s.row_ready, 1)
                n_row += 1
        for t in range(TT):
            if t == 0:
                act.wait_ge(s.ada0, 1)
            affine(t, HT0, 0, 0)
            if t + 2 < TT:
                u = t + 2
                act.wait_ge(s.xt0 if u % 2 == 0 else s.xt1, 16 * (u // 2 + 1) if u < L else 16 * (L // 2 + L))
                stats(u, XS[u % 2][:], SQ0[:], 0)
            round_hi(t, HT0, 0)
            if t < 2:
                split_hi(t, FIRST_IN + t)
        uds = [s.ud_w0, s.ud_w1, s.ud_w2, s.ud_w3]
        a = 0
        for mb in range(KB):
            for g in range(NG):
                act.wait_ge(s.mm_act, a + 1)
                src = BANK[a % 4][:, 0:TG]
                if mb < 4:
                    if a == 0:
                        act.wait_ge(s.tabs, 4)
                    dst = POOL[:, mb, :]
                    dl = dst[:, 0:LAT].rearrange("p (c j) -> p j c", j=L)
                    if g < 2:
                        S.activation(dl[:, 3 * g:3 * g + 3, :], src.rearrange("p (j c) -> p j c", c=CL), ACT.Copy).then_inc(s.ev_act, 1)
                    else:
                        S.activation(dl[:, 6:8, :], src[:, 0:256].rearrange("p (j c) -> p j c", c=CL), ACT.Copy).then_inc(s.acts, 1)
                        S.activation(dst[:, LAT:T].rearrange("p (c j) -> p j c", j=L),
                                     src[:, 256:384].rearrange("p (j c) -> p j c", c=CC), ACT.Copy).then_inc(s.ev_act, 1)
                else:
                    if mb >= 6:
                        act.wait_ge(uds[mb - 6], 16)
                    if a == 12:
                        act.wait_ge(s.h_lo, TT)
                    S.activation(PROJ[mb % 2][:, g * TG:(g + 1) * TG], src, ACT.Copy).then_inc(s.ev_act, 1)
                a += 1
            if mb >= 4:
                act.wait_ge(s.ev_act, a)
                act.dma_start(UD[(mb - 4) * P:(mb - 3) * P, :], PROJ[mb % 2][:]).then_inc(uds[mb - 4], 16)
            if mb == 4:
                for b in range(16):
                    act.wait_ge(s.wbt_mm, b + 1)
                    S.activation(WB[:, 4 * b:4 * b + 4, :].rearrange("p q c -> p (q c)"), BANK[6 + b % 2][:], ACT.Copy)\
                     .then_inc(s.wb_ready, 1)
            if mb + 2 < KB:
                split_hi(mb + 2, FIRST_IN + mb + 2)
        act.wait_ge(s.mm_act, 24)
        for b in range(32):
            g0, d = 2 * (b // 2), b % 2
            act.wait_ge(s.mm_act, a + 1)
            src = BANK[a % 4][:, 0:2 * CH].rearrange("p (g c) -> p g c", g=2)
            hs = H[:, d, g0:g0 + 2, :]
            fin = FIN[:, d * G + g0:d * G + g0 + 2].unsqueeze(2)
            if d == 0:
                S.activation(hs[:, :, 1:CL], src[:, :, 0:CL - 1], ACT.Copy).then_inc(s.acts, 1)
                S.activation(hs[:, :, CL + 1:CH], src[:, :, CL:CH - 1], ACT.Copy).then_inc(s.acts, 1)
                S.activation(fin, src[:, :, CH - 1:CH], ACT.Copy).then_inc(s.ev_act, 1)
            else:
                S.activation(hs[:, :, CL - 1:0:-1], src[:, :, 1:CL], ACT.Copy).then_inc(s.acts, 1)
                S.activation(hs[:, :, CH - 1:CL:-1], src[:, :, CL + 1:CH], ACT.Copy).then_inc(s.acts, 1)
                S.activation(fin, src[:, :, CL:CL + 1], ACT.Copy).then_inc(s.ev_act, 1)
            a += 1
        for b in range(8):
            act.wait_ge(s.c_mm, b + 1)
            src = BANK[6 + b % 2]
            S.activation(C1[:, 8 * b:8 * b + 8, :].rearrange("p q c -> p (q c)"), src[:, 0:P], ACT.Copy, scale=CSG[:])\
             .then_inc(s.c_ready, 1)
            S.activation(C2[:, 8 * b:8 * b + 8, :].rearrange("p q c -> p (q c)"), src[:, P:2 * P], ACT.Copy, scale=-1.0)\
             .then_inc(s.c_ready, 1)
        act.dma_start(BIAS2[:], b_ada[:, 2 * D:2 * D + 512]).then_inc(s.bias2_in, 16)
        for k in range(8):
            part, hf = k // 2, k % 2
            act.wait_ge(s.ada_mm, 3 + k)
            if k < 7:
                act.dma_start(BIAS2[:], b_ada[:, 2 * D + 512 * (k + 1):2 * D + 512 * (k + 2)]).then_inc(s.bias2_in, 16)
            if k in (1, 2, 7):
                act.wait_ge(s.gates_w, {1: 16, 2: 32, 7: 48}[k])
            S.activation(ROW2[:], BANK[4 + k % 2][0:2, :], ACT.Copy).then_inc(s.row_ready, 1)
            if part in (0, 3):
                act.wait_ge(s.row_ready, 5 + k)
                act.dma_start(GD[part // 3, :, hf * 512:hf * 512 + 512], ROW2[:]).then_inc(s.gates_w, 16)
            else:
                act.wait_ge(s.ada_cols, 3 + k)
                cols = BANK[7][:, 64 + 8 * (k % 4):72 + 8 * (k % 4)].rearrange("p (k a) -> p a k", a=2)
                dst = ADA[3 if part == 1 else 2][:, :, 4 * hf:4 * hf + 4]
                S.activation(dst, cols, ACT.Copy).then_inc(s.acts, 1)
        act.wait_ge(uds[2], 16)
        mdw = [s.md_w0, s.md_w1]

        def map_out(i, a):
            gi, g = i // NG, i % NG
            act.wait_ge(s.mm_act, a + 1)
            if i >= 2:
                act.wait_ge(mdw[i % 2], 16 * (i // 2))
            S.activation(EST[i % 2][:], BANK[a % 4][:, 0:TG], ACT.Copy, scale=COL[:, 32 + gi:33 + gi]).then_inc(s.ev_act, 1)
            act.wait_ge(s.ev_act, a + 1)
            act.dma_start(MD[gi * P:(gi + 1) * P, g * TG:(g + 1) * TG], EST[i % 2][:]).then_inc(mdw[i % 2], 16)
        for i in range(DVE_WINDOWS * NG):
            map_out(i, a)
            a += 1
        for b in range(16):
            act.wait_ge(s.kk_mm, b + 1)
            S.activation(KK[:, 2 * b:2 * b + 2].rearrange("p g e c -> p (g e c)"), BANK[6 + b % 2][0:SP, 0:480], ACT.Copy)\
             .then_inc(s.kk_ready, 1)
        for i in range(DVE_WINDOWS * NG, 12):
            map_out(i, a)
            a += 1
        act.wait_ge(s.mm_act, 68)
        for b in range(16):
            act.wait_ge(s.mm_act, a + 1)
            S.activation(Y[:, 2 * b:2 * b + 2, :].rearrange("p g c -> p (g c)"), BANK[a % 4][:, 0:2 * CH], ACT.Gelu_apprx_tanh)\
             .then_inc(s.ev_act, 1)
            a += 1
        for w in range(2):
            split_hi(N_IN + w, FIRST_GLU + w)
        for g, q in enumerate((s.yr0, s.yr1, s.yr2)):
            act.wait_ge(q, 16)
            if g:
                act.wait_ge(s.mm_act, 84 + 4 * g)
            S.activation(YH[:], YR[:, :, g * TG:(g + 1) * TG], ACT.Copy).then_inc(s.y_split_hi, 1)
            act.wait_ge(s.mp_in, 16 * (g + 1))
            S.activation(XH[:, 0:4, g * TG:(g + 1) * TG], MP[:], ACT.Copy).then_inc(s.mix_hi, 1)
            for m in range(4):
                act.wait_ge(s.mm_act, a + 1)
                if a - 84 >= 2:
                    act.wait_ge(s.so, a - 84 - 1)
                S.activation(SZ[a % 2][:], BANK[a % 4][:, 0:TG], ACT.Sigmoid).then_inc(s.ev_act, 1)
                a += 1
            if g == 0:
                for w in range(2, 4):
                    split_hi(N_IN + w, FIRST_GLU + w)
        assert a == A_STRAIGHT
        for w in range(4, N_GLU + N_OUT + 2):
            split_hi(N_IN + w, FIRST_GLU + w)
        W1 = N_IN + N_GLU + N_OUT
        for t in range(1, TT + LAG):
            u = t - 1
            if u < TT:
                act.wait_ge(s.acc, B_STRAIGHT - 18 + 2 * (u + 1))
                stats(u, ACC[:, u, :], SQ1[:], TT)
            if t >= LAG:
                affine(t - LAG, HT1, 2, TT)
                round_hi(t - LAG, HT1, TT)

        def w_hi_loop(ch, i, ahead):
            w, n = W1 + i + 4 * ahead, FIRST_MLP + i + 4 * ahead
            act.wait_ge(raw_in[n % 4], ch * 16 + 16 * (n // 4 + 1))
            if i >= 2:
                act.wait_ge(s.mm_dve, ch * 18 + B_STRAIGHT)
            else:
                act.wait_ge(s.mm_act, ch * 6 + (A_STRAIGHT + 6))
            S.activation(WH[w_slot(w)][:], RAW[n % 4][:], ACT.Copy).then_inc(s.w_hi, 1)

        def act_chunk(ch, last=False):
            for i in range(6):
                if i in (2, 3):
                    w_hi_loop(ch, i, 0)
                act.wait_ge(s.mm_act, ch * 6 + (A_STRAIGHT + i + 1))
                if i >= 2:
                    act.wait_ge(s.f_ready, ch * 6 + (i - 1))
                S.activation(RL[i % 2][:], BANK[i % 4][:, 0:TG], ACT.Relu).then_inc(s.ev_act, 1)
            if not last:
                for i in range(2):
                    w_hi_loop(ch, i, 1)

        with act.Fori(0, NFC - 1) as ch:
            act_chunk(ch)
        act_chunk(NFC - 1, last=True)
        for t in range(TT):
            act.wait_ge(s.acc, B_STRAIGHT + 18 * (NFC - 1) + 2 * (t + 1))
            if t:
                act.wait_ge(s.sq, 2 * TT + t)
            stats(t, ACC[:, t, :], SQ[:], 2 * TT)

    @block.vector
    def _(dve):
        count = [0]

        def then(ins):
            count[0] += 1
            ins.then_inc(s.dve, 1)
            dve.wait_ge(s.dve, count[0])

        tt, ts, stt = V.tensor_tensor, V.tensor_scalar, V.scalar_tensor_tensor
        then(V.memset(PR[:, 0, :], 1.0))
        V.memset(PI[:, 0, :], 0.0).then_inc(s.tabs, 1)
        V.memset(EPSB[:], EPS).then_inc(s.tabs, 1)
        then(V.memset(CSG[0:N, :], 1.0))
        then(V.memset(CSG[N:P, :], -1.0))
        dve.wait_ge(s.tab_dt, 1)
        then(ts(M1[:], AR[:], DT[:], None, ALU.mult))
        then(ts(TH[:], AI[:], DT[:], None, ALU.mult))
        then(ts(KT[:], TH[:], 0.15915494309189535, MAGIC, ALU.mult, ALU.add))
        V.tensor_scalar(KT[:], KT[:], MAGIC, None, ALU.subtract).then_inc(s.tab_th, 1)
        dve.wait_ge(s.tab_th, 1)
        then(stt(RT[:], KT[:], -TWO_PI[0], TH[:], ALU.mult, ALU.add))
        then(stt(RT[:], KT[:], -TWO_PI[1], RT[:], ALU.mult, ALU.add))
        then(stt(RT[:], KT[:], -TWO_PI[2], RT[:], ALU.mult, ALU.add))
        ts(RT[:], RT[:], 3.1415925, -3.1415925, ALU.min, ALU.max).then_inc(s.tab_th, 1)
        dve.wait_ge(s.pe_small, 1)
        V.tensor_copy(COL[:], BANK[7][:, 0:36]).then_inc(s.col_ready, 1)
        dve.wait_ge(s.tab_sin, 2)
        then(tt(C0[:], SH[:], SH[:], ALU.mult))
        then(ts(C0[:], C0[:], -2.0, 1.0, ALU.mult, ALU.add))
        dve.wait_ge(s.tab_e, 1)
        then(tt(TAB[:, 0, 0:N], EX[:], C0[:], ALU.mult))
        then(tt(TAB[:, 1, 0:N], EX[:], SR[:], ALU.mult))
        then(ts(NR[:], TAB[:, 0, 0:N], 1.0, None, ALU.subtract))
        then(tt(M1[:], AR[:], AR[:], ALU.mult))
        then(tt(M2[:], AI[:], AI[:], ALU.mult))
        then(tt(DEN[:], M1[:], M2[:], ALU.add))
        then(V.reciprocal(RD[:], DEN[:]))
        then(tt(M1[:], NR[:], AR[:], ALU.mult))
        then(tt(M2[:], TAB[:, 1, 0:N], AI[:], ALU.mult))
        then(tt(M3[:], TAB[:, 1, 0:N], AR[:], ALU.mult))
        then(tt(M4[:], NR[:], AI[:], ALU.mult))
        then(tt(M1[:], M1[:], M2[:], ALU.add))
        then(tt(M3[:], M3[:], M4[:], ALU.subtract))
        then(tt(TAB[:, 2, 0:N], M1[:], RD[:], ALU.mult))
        then(tt(TAB[:, 3, 0:N], M3[:], RD[:], ALU.mult))
        V.tensor_copy(TAB[:, :, N:P], TAB[:, :, 0:N]).then_inc(s.tabs, 1)
        dve.wait_ge(s.pe_small, 2)
        tb = BANK[6][:, 0:4 * Q].rearrange("p (i q) -> p i q", i=4)
        then(V.tensor_copy(PR[:, 1, :], tb[:, 0, :]))
        then(V.tensor_copy(PI[:, 1, :], tb[:, 1, :]))
        then(V.tensor_copy(ZR[:], tb[:, 2, :]))
        then(V.tensor_copy(ZI[:], tb[:, 3, :]))
        dve.wait_ge(s.sgn_ready, 2)
        then(ts(ZS[:], ZI[:], SGN[:], None, ALU.mult))
        then(ts(ZT[:], ZR[:], SGN[:], None, ALU.mult))
        then(ts(ZU[:], ZI[:], -1.0, None, ALU.mult))
        for n in (1, 2, 4):
            br = PR[:, n, :].unsqueeze(1).to_broadcast([P, n, Q])
            bi = PI[:, n, :].unsqueeze(1).to_broadcast([P, n, Q])
            lo, hi = slice(1, n + 1), slice(n + 1, 2 * n + 1)
            then(tt(PR[:, hi, :], PR[:, lo, :], br, ALU.mult))
            then(tt(PT[0][:, 0:n, :], PI[:, lo, :], bi, ALU.mult))
            then(tt(PI[:, hi, :], PR[:, lo, :], bi, ALU.mult))
            then(tt(PT[1][:, 0:n, :], PI[:, lo, :], br, ALU.mult))
            then(tt(PR[:, hi, :], PR[:, hi, :], PT[0][:, 0:n, :], ALU.subtract))
            then(tt(PI[:, hi, :], PI[:, hi, :], PT[1][:, 0:n, :], ALU.add))
        dve.wait_ge(s.b_in, 64)

        def zq(z):
            return z[:].unsqueeze(2).to_broadcast([P, Q, SP])

        then(tt(B1[:], BX[:], zq(ZR), ALU.mult))
        then(tt(TB[:], BY[:], zq(ZS), ALU.mult))
        then(tt(B1[:], B1[:], TB[:], ALU.add))
        then(tt(B2[:], BY[:], zq(ZT), ALU.mult))
        then(tt(TB[:], BX[:], zq(ZU), ALU.mult))
        tt(B2[:], B2[:], TB[:], ALU.add).then_inc(s.tabs, 1)
        dve.wait_ge(s.tabs, 4)

        def to_state(d, j0):
            q0 = d * G
            for j in range(j0, j0 + 4):
                e = L - 1 - j if d == 0 else j
                out = WB[:, q0:q0 + G, j * SP:(j + 1) * SP]
                pr = PR[:, e, q0:q0 + G].unsqueeze(2).to_broadcast([P, G, SP])
                pi = PI[:, e, q0:q0 + G].unsqueeze(2).to_broadcast([P, G, SP])
                tt(out, B1[:, q0:q0 + G, :], pr, ALU.mult).then_inc(s.dve, 1)
                tt(TW[j % 2][:], B2[:, q0:q0 + G, :], pi, ALU.mult).then_inc(s.dve, 1)
                count[0] += 2
                dve.wait_ge(s.dve, count[0])
                tt(out, out, TW[j % 2][:], ALU.add).then_inc(s.wbt, 1)
                dve.wait_ge(s.wbt, d * L + j + 1)

        def normed(t, src, dst, base):
            dve.wait_ge(s.root, base + t + 1)
            then(V.reciprocal(STAT[2][:, t:t + 1], STAT[1][:, t:t + 1]))
            ts(dst, src, STAT[2][:, t:t + 1], None, ALU.mult).then_inc(s.xn, 1)

        def affine(t, ht, ada, base):
            cond = 0 if t < L else 1
            dve.wait_ge(s.tr, base + t + 1)
            if base + t >= 2:
                dve.wait_ge(s.h_lo, base + t - 1)
            for k in range(4):
                ts(ht[t % 2][:, k, :], turn_banks(t, 6 if base else 2)[0][:, k * P:(k + 1) * P], ADA[ada][:, cond, k:k + 1],
                   ADA[ada + 1][:, cond, k:k + 1], ALU.mult, ALU.add).then_inc(s.aff_d, 1)

        def round_lo(t, ht, base):
            dve.wait_ge(s.h_hi, base + t + 1)
            tt(XL[:, :, t * P:(t + 1) * P], ht[t % 2][:], XH[:, :, t * P:(t + 1) * P].bitcast(F32), ALU.subtract).then_inc(s.h_lo, 1)

        def split_lo(w, n):
            dve.wait_ge(s.w_hi, w + 1)
            tt(WL[w_slot(w)][:], RAW[n % 4][:], WH[w_slot(w)][:].bitcast(F32), ALU.subtract).then_inc(s.w_split, 1)

        def ada_scale(dst, cols, norm, hf):
            for cond in range(2):
                then(stt(dst[:, cond, 4 * hf:4 * hf + 4], cols[:, cond, :], 1.0,
                         COL[:, norm + 4 * hf:norm + 4 * hf + 4], ALU.add, ALU.mult))

        normed(0, XS[0][:], XS[0][:], 0)
        normed(1, XS[1][:], XS[1][:], 0)
        dve.wait_ge(s.ada_cols, 4)
        for k in range(4):
            cols = BANK[7][:, 64 + 8 * k:72 + 8 * k].rearrange("p (k a) -> p a k", a=2)
            if k < 2:
                ada_scale(ADA[0], cols, 16, k)
            else:
                then(V.tensor_copy(ADA[1][:, :, 4 * (k - 2):4 * (k - 2) + 4], cols))
        V.tensor_copy(AQ[:], PI[:, L, :]).then_inc(s.ada0, 1)
        dve.wait_ge(s.ada0, 1)
        for t in range(TT):
            if t >= 1 and t + 1 < TT:
                normed(t + 1, XS[(t + 1) % 2][:], XS[(t + 1) % 2][:], 0)
            affine(t, HT0, 0, 0)
            round_lo(t, HT0, 0)
            if t < 2:
                split_lo(t, FIRST_IN + t)
        for w in range(2, N_IN):
            if w < 6:
                to_state((w - 2) // 2, w % 2 * 4)
            split_lo(w, FIRST_IN + w)
        then(ts(AQ[N:P, :], PI[N:P, L, :], -1.0, None, ALU.mult))
        dve.wait_ge(s.st_in, 16)
        V.tensor_copy(STR[:], ST[:].rearrange("q n r -> q r n")).then_inc(s.h0_mm, 1)
        pool_window(dve, tt, then, V.tensor_copy, 0)
        dve.wait_ge(s.mm_act, 24)
        dve.wait_ge(s.pe_small, 3)
        h0 = BANK[6][:, 0:Q]
        for d in range(2):
            V.tensor_copy(H[:, d, :, 0], h0[:, d * G:(d + 1) * G]).then_inc(s.h_init, 1)
        for d in range(2):
            V.memset(H[:, d, :, CL], 0.0).then_inc(s.h_init, 1)
        for gi in range(1, DVE_WINDOWS):
            pool_window(dve, tt, then, V.tensor_copy, gi)

        dve.wait_ge(s.ev_act, 56)
        dve.wait_ge(s.h_init, 4)
        row = 2 * G * CH
        lat = [bass.AP(H, p0 * row, [[row, n], [0, 1], [CH, Q], [1, CL]]) for p0, n in ((0, P), (0, N), (N, N))]
        both = [bass.AP(H, p0 * row, [[row, n], [CL, 2], [CH, Q], [1, CC]]) for p0, n in ((0, P), (0, N), (N, N))]

        def at_slot(v, i):
            return v[:, :, :, bass.ds(i, 1)] if not isinstance(i, int) else v[:, :, :, i:i + 1]

        def products(v, i, n):
            full, top, bot = v
            if not isinstance(i, int) or i:
                dve.wait_ge(s.sc_h, i)
            ar = PR[:, L, :].unsqueeze(1).to_broadcast([P, n, Q]).unsqueeze(3)
            ai = AQ[:].unsqueeze(1).to_broadcast([P, n, Q]).unsqueeze(3)
            tt(PS_[:, 0:n].unsqueeze(3), at_slot(full, i), ar, ALU.mult).then_inc(s.sc_p, 1)
            tt(QS_[0:N, 0:n].unsqueeze(3), at_slot(bot, i), ai[N:P], ALU.mult).then_inc(s.sc_p, 1)
            tt(QS_[N:P, 0:n].unsqueeze(3), at_slot(top, i), ai[0:N], ALU.mult).then_inc(s.sc_p, 1)

        def step(v, i, n):
            products(v, i, n)
            dst = at_slot(v[0], i + 1)
            dve.wait_ge(s.sc_p, i * 3 + 1)
            tt(RS_[:, 0:n].unsqueeze(3), PS_[:, 0:n].unsqueeze(3), dst, ALU.add).then_inc(s.sc_r, 1)
            dve.wait_ge(s.sc_p, i * 3 + 3)
            dve.wait_ge(s.sc_r, i + 1)
            tt(dst, RS_[:, 0:n].unsqueeze(3), QS_[:, 0:n].unsqueeze(3), ALU.add).then_inc(s.sc_h, 1)

        step(both, 0, 2)
        half = (CC - 2) // 2
        with dve.Fori(1, half + 2, half) as i:
            for k in range(half):
                step(both, i + k, 2)
        i = CC - 1
        products(both, i, 2)
        dve.wait_ge(s.sc_p, i * 3 + 3)
        dst = at_slot(lat[0], i + 1)
        tt(RS_[:, 0:1].unsqueeze(3), PS_[:, 0:1].unsqueeze(3), dst, ALU.add).then_inc(s.sc_r, 1)
        tt(RS_[:, 1], PS_[:, 1], FIN[:], ALU.add).then_inc(s.cx_r, 1)
        dve.wait_ge(s.sc_r, i + 1)
        tt(dst, RS_[:, 0:1].unsqueeze(3), QS_[:, 0:1].unsqueeze(3), ALU.add).then_inc(s.sc_h, 1)
        dve.wait_ge(s.cx_r, 1)
        tt(FIN[:], RS_[:, 1], QS_[:, 1], ALU.add).then_inc(s.cx_h, 1)
        unroll = 12
        rounds = (CL - 1 - CC) // unroll
        with dve.Fori(CC, CC + (rounds - 1) * unroll + 1, unroll) as i:
            for k in range(unroll):
                step(lat, i + k, 1)
        for i in range(CC + rounds * unroll, CL - 1):
            step(lat, i, 1)
        dve.wait_ge(s.acts, 4 + 64 + 4)
        for cond in range(2):
            then(stt(ADA[2][:, cond, :], ADA[2][:, cond, :], 1.0, COL[:, 24:32], ALU.add, ALU.mult))
        dve.wait_ge(s.fin_mm, 1)
        dve.wait_ge(s.h0_mm, 1)
        V.tensor_copy(ST[:], BANK[6][0:Q, 0:P].rearrange("q (r n) -> q n r", r=2)).then_inc(s.fin_ready, 1)
        for w in range(2):
            split_lo(N_IN + w, FIRST_GLU + w)
        a = 0
        for g in range(NG):
            cols = slice(g * TG, (g + 1) * TG)
            dve.wait_ge(s.y_split_hi, g + 1)
            tt(YL[:], YR[:, :, cols], YH[:].bitcast(F32), ALU.subtract).then_inc(s.y_split, 1)
            dve.wait_ge(s.mix_hi, g + 1)
            tt(XL[:, 0:4, cols], MP[:], XH[:, 0:4, cols].bitcast(F32), ALU.subtract).then_inc(s.mix_pool, 1)
            for m in range(4):
                dve.wait_ge(s.ev_act, 84 + a + 1)
                if a:
                    dve.wait_ge(s.mix_ready, a)
                tt(SO[:], SZ[a % 2][:], YR[:, m, cols], ALU.mult).then_inc(s.so, 1)
                dve.wait_ge(s.so, a + 1)
                then(V.tensor_copy(XH[:, 4 + m, cols], SO[:]))
                tt(XL[:, 4 + m, cols], SO[:], XH[:, 4 + m, cols].bitcast(F32), ALU.subtract).then_inc(s.mix_ready, 1)
                a += 1
            if g == 0:
                for w in range(2, 4):
                    split_lo(N_IN + w, FIRST_GLU + w)
        dve.wait_ge(s.gb_in, 16)
        dve.wait_ge(s.mix_ready, 12)
        def gate_out(i):
            o_ = i % 18
            if o_ in (2, 8):
                w = 4 + 2 * (i // 18) + (0 if o_ == 2 else 1)
                split_lo(N_IN + w, FIRST_GLU + w)
            cond = 0 if o_ // 2 < L else 1
            dve.wait_ge(s.mm_dve, i + 1)
            if i >= 4:
                dve.wait_ge(s.acc, i - 3)
            tt(BT3[i % 4][:], BANK[i % 4][:], GB[:, cond, (o_ % 2) * 512:(o_ % 2) * 512 + 512], ALU.mult).then_inc(s.ev_dve, 1)

        for i in range(B_STRAIGHT - 18):
            gate_out(i)
        W1 = N_IN + N_GLU + N_OUT
        for t in range(TT + LAG):
            if t < TT:
                for n in range(2):
                    gate_out(B_STRAIGHT - 18 + 2 * t + n)
            u = t - 1
            if 0 <= u < TT:
                if u >= 2:
                    dve.wait_ge(s.tr, TT + u - 1)
                normed(u, ACC[:, u, :], XN[u % 2][:], TT)
            if t >= LAG:
                affine(t - LAG, HT1, 2, TT)
                round_lo(t - LAG, HT1, TT)
        dve.wait_ge(s.h_lo, 2 * TT)
        dve.wait_ge(s.acc, B_STRAIGHT)

        def lo_loop(ch, i, ahead):
            w, n = W1 + i + 4 * ahead, FIRST_MLP + i + 4 * ahead
            dve.wait_ge(s.w_hi, ch * 4 + (w + 1))
            tt(WL[w_slot(w)][:], RAW[n % 4][:], WH[w_slot(w)][:].bitcast(F32), ALU.subtract).then_inc(s.w_split, 1)

        def square(ch, i):
            g, m = i // 2, i % 2
            cols = slice(g * TG, (g + 1) * TG)
            dve.wait_ge(s.ev_act, ch * 6 + (A_STRAIGHT + i + 1))
            dve.wait_ge(s.mm_dve, ch * 18 + (B_STRAIGHT - 18 + 6 * (g + 1)))
            if i >= 2:
                dve.wait_ge(s.f_ready, ch * 6 + (i - 1))
            tt(FT[i % 2][:], RL[i % 2][:], RL[i % 2][:], ALU.mult).then_inc(s.sqr, 1)
            dve.wait_ge(s.sqr, ch * 12 + (2 * i + 1))
            V.tensor_copy(FH[:, m, cols], FT[i % 2][:]).then_inc(s.sqr, 1)
            dve.wait_ge(s.sqr, ch * 12 + (2 * i + 2))
            tt(FL[:, m, cols], FT[i % 2][:], FH[:, m, cols].bitcast(F32), ALU.subtract).then_inc(s.f_ready, 1)

        def gate(ch, i):
            cond = 0 if i // 2 < L else 1
            dve.wait_ge(s.mm_dve, ch * 18 + (B_STRAIGHT + i + 1))
            dve.wait_ge(s.acc, ch * 18 + (B_STRAIGHT + max(i - 3, 0)))
            tt(BT[i % 4][:], BANK[(6 + i) % 4][:], GB[:, cond, (i % 2) * 512:(i % 2) * 512 + 512], ALU.mult).then_inc(s.ev_dve, 1)

        dve.wait_ge(s.gb_in, 32)

        def chunk(ch, last=False):
            for i in range(6):
                square(ch, i)
                if i in (3, 4):
                    lo_loop(ch, i - 1, 0)
            for i in range(18):
                gate(ch, i)
                if not last and i in (2, 6):
                    lo_loop(ch, 0 if i == 2 else 1, 1)
                if last and i >= 5 and i % 2 == 1:
                    final(i // 2 - 2)

        def final(t):
            dve.wait_ge(s.root, 2 * TT + t + 1)
            then(V.reciprocal(STAT[2][:, t:t + 1], STAT[1][:, t:t + 1]))
            stt(ACC[:, t, :], ACC[:, t, :], STAT[2][:, t:t + 1], NO[:], ALU.mult, ALU.mult).then_inc(s.y_final, 1)

        with dve.Fori(0, NFC - 1) as ch:
            chunk(ch)
        dve.wait_ge(s.no_in, 16)
        chunk(NFC - 1, last=True)
        final(TT - 2)
        final(TT - 1)

    @block.tensor
    def _(pe):
        mm = PE.matmul

        def three(out, stat, mov, first, last):
            (sh_, sl), (mh, ml) = stat, mov
            mm(out, sh_, mh, start=first, stop=False)
            mm(out, sh_, ml, start=False, stop=False)
            return mm(out, sl, mh, start=False, stop=last)

        pe.wait_ge(s.vec_in, 80)
        pe.wait_ge(s.id_ready, 1)
        PE.transpose(BANK[7][:, 0:36], VEC[:], ID[0:36, 0:36]).then_inc(s.pe_small, 1)

        def ada_unit(n, banks, k):
            raw_landed(pe, n)
            cv = COL[:, 0:16].rearrange("p (a k) -> p a k", a=2)[:, :, k]
            for hf in range(2):
                last = mm(BANK[banks[hf]][0:2, :], cv, RAW[n % 4][:, hf * 512:hf * 512 + 512], start=(k == 0), stop=False)
            last.then_inc(s.ada_used, 1)

        pe.wait_ge(s.silu_done, 1)
        pe.wait_ge(s.bias0_in, 32)
        pe.wait_ge(s.sgn_ready, 3)
        for part in range(2):
            for k in range(KB):
                ada_unit(part * KB + k, (2 * part, 2 * part + 1), k)
            for hf in range(2):
                last = mm(BANK[2 * part + hf][0:2, :], ONE[:], BIAS0[:, part * D + hf * 512:part * D + hf * 512 + 512],
                          start=False, stop=True)
            last.then_inc(s.ada_mm, 1)
            if part == 0:
                pe.wait_ge(s.tabs, 3)
                for i in range(4):
                    last = PE.transpose(BANK[6][:, i * Q:(i + 1) * Q], TAB[:, i, :], ID[0:Q, 0:Q])
                last.then_inc(s.pe_small, 1)
        for k in range(4):
            pe.wait_ge(s.row_ready, k + 1)
            for i in range(4):
                last = PE.transpose(BANK[7][:, 64 + 8 * k + 2 * i:66 + 8 * k + 2 * i], ROW0[:, i * P:(i + 1) * P], ID[0:2, 0:2])
            last.then_inc(s.ada_cols, 1)

        def turn_tile(t, src, base):
            pe.wait_ge(s.xn, base + t + 1)
            if t >= 2:
                pe.wait_ge(s.aff_d, 4 * (base + t - 1))
                pe.wait_ge(s.aff_a, 4 * (base + t - 1))
            for k in range(KB):
                last = PE.transpose(turn_banks(t, 6 if base else 2)[k // 4][:, (k % 4) * P:(k % 4 + 1) * P], src[:, k * P:(k + 1) * P], ID[:])
            last.then_inc(s.tr, 1)

        for t in range(TT):
            turn_tile(t, XS[t % 2], 0)

        a = 0

        def bank_free(a):
            if a >= 4:
                pe.wait_ge(s.ev_act, a - 3)
            else:
                pe.wait_ge(s.row_ready, a + 1)

        for mb in range(KB):
            pe.wait_ge(s.w_split, mb + 1)
            wh = WH[mb % 2][:].rearrange("p (k f) -> p k f", k=KB)
            wl = WL[mb % 2][:].rearrange("p (k f) -> p k f", k=KB)
            for g in range(NG):
                if mb == 0:
                    pe.wait_ge(s.h_lo, 3 * (g + 1))
                bank_free(a)
                for k in range(KB):
                    last = three(BANK[a % 4][:, 0:TG], (wh[:, k], wl[:, k]),
                                 (XH[:, k, g * TG:(g + 1) * TG], XL[:, k, g * TG:(g + 1) * TG]), k == 0, k == KB - 1)
                last.then_inc(s.mm_act, 1)
                a += 1
            if mb == 4:
                pe.wait_ge(s.wbt, 16)
                for b in range(16):
                    if b >= 2:
                        pe.wait_ge(s.wb_ready, b - 1)
                    for i in range(4):
                        last = PE.transpose(BANK[6 + b % 2][:, i * P:(i + 1) * P], WB[:, 4 * b + i, :], ID[:])
                    last.then_inc(s.wbt_mm, 1)
        for b in range(32):
            g0, d = 2 * (b // 2), b % 2
            if b == 0:
                pe.wait_ge(s.wb_ready, 16)
                pe.wait_ge(s.u_in0, 16 * 16)
            if b == 16:
                pe.wait_ge(s.u_in1, 16 * 16)
            bank_free(a)
            for i in range(2):
                last = mm(BANK[a % 4][:, i * CH:(i + 1) * CH], WB[:, d * G + g0 + i, :], U[:, g0 + i, :], start=True, stop=True)
            last.then_inc(s.mm_act, 1)
            a += 1
            if b == 3:
                pe.wait_ge(s.h0_mm, 1)
                PE.transpose(BANK[6][:, 0:Q], STR[:].rearrange("q r n -> q (r n)"), ID[0:Q, 0:Q]).then_inc(s.pe_small, 1)
        for b in range(8):
            if b == 0:
                pe.wait_ge(s.cs_in, 48)
                pe.wait_ge(s.h_init, 2)
            if b >= 2:
                pe.wait_ge(s.c_ready, 2 * (b - 1))
            PE.transpose(BANK[6 + b % 2][:, 0:P], CS[:, b, 0:2, :].rearrange("p k n -> p (k n)"), ID[:])
            PE.transpose(BANK[6 + b % 2][:, P:2 * P], CS[:, b, 1:3, :].rearrange("p k n -> p (k n)"), ID[:]).then_inc(s.c_mm, 1)
        for part in range(4):
            for k in range(KB):
                n = FIRST_ADA2 + part * KB + k
                raw_landed(pe, n)
                if k == 0:
                    if part:
                        pe.wait_ge(s.row_ready, 4 + 2 * part)
                    else:
                        pe.wait_ge(s.aff_a, 4 * TT)
                        pe.wait_ge(s.aff_d, 4 * TT)
                cv = COL[:, 0:16].rearrange("p (a k) -> p a k", a=2)[:, :, k]
                for hf in range(2):
                    last = mm(BANK[4 + hf][0:2, :], cv, RAW[n % 4][:, hf * 512:hf * 512 + 512], start=(k == 0), stop=False)
                last.then_inc(s.ada_used, 1)
            for hf in range(2):
                pe.wait_ge(s.bias2_in, 16 * (2 * part + hf + 1))
                mm(BANK[4 + hf][0:2, :], ONE[:], BIAS2[:], start=False, stop=True).then_inc(s.ada_mm, 1)
                if part in (1, 2):
                    k_ = 2 * part + hf
                    pe.wait_ge(s.row_ready, 5 + k_)
                    if k_ == 2:
                        pe.wait_ge(s.c_ready, 16)
                    else:
                        pe.wait_ge(s.acts, 68 + k_ - 2)
                    for i in range(4):
                        o = 64 + 8 * (k_ % 4) + 2 * i
                        last = PE.transpose(BANK[7][:, o:o + 2], ROW2[:, i * P:(i + 1) * P], ID[0:2, 0:2])
                    last.then_inc(s.ada_cols, 1)
        def channel_map(i, a):
            gi, g = i // NG, i % NG
            bank_free(a)
            pe.wait_ge(s.pooled, gi + 1)
            out, src = BANK[a % 4], POOL[:, gi, :]
            lat = src[:, 0:LAT].rearrange("p (c j) -> p j c", j=L)
            if g < 2:
                last = mm(lat_j3(out[:, 0:TG]), PWS[:, gi, :], lat[:, 3 * g:3 * g + 3, :], start=True, stop=True)
            else:
                mm(lat_j3(out[:, 0:256]), PWS[:, gi, :], lat[:, 6:8, :], start=True, stop=True)
                last = mm(out[:, 256:384].rearrange("p (j c) -> p j c", c=CC), PWS[:, gi, :],
                          src[:, LAT:T].rearrange("p (c j) -> p j c", j=L), start=True, stop=True)
            last.then_inc(s.mm_act, 1)

        pe.wait_ge(s.pw_in, 16)
        for i in range(DVE_WINDOWS * NG):
            channel_map(i, a)
            a += 1
        pe.wait_ge(s.ca_ready, 16)
        pe.wait_ge(s.dd_ready, 1)
        for b in range(16):
            if b >= 2:
                pe.wait_ge(s.kk_ready, b - 1)
            else:
                pe.wait_ge(s.acts, 72)
            for i in range(2):
                g = 2 * b + i
                o = BANK[6 + b % 2][0:SP, i * 240:(i + 1) * 240]
                mm(o[:, 0:112], B1[:, G + g, :], CA[:, G + g, SP:P], start=(i == 0), stop=False, skip_group_check=True)
                mm(o[:, 112:128], B1[:, G + g, :], C1[:, G + g, :], start=False, stop=False, skip_group_check=True)
                mm(o[:, 112:128], B1[:, g, :], C1[:, g, :], start=False, stop=False, skip_group_check=True)
                mm(o[:, 112:128], ID[0:SP, 0:SP], DD[:, g, :], start=False, stop=True, skip_group_check=True)
                last = mm(o[:, 128:240], B1[:, g, :], CA[:, g, 0:112], start=False, stop=True, skip_group_check=True)
            last.then_inc(s.kk_mm, 1)
        for i in range(DVE_WINDOWS * NG, 12):
            channel_map(i, a)
            a += 1
        pe.wait_ge(s.loc_in, 16 * L)
        pe.wait_ge(s.sc_h, CL - 1)
        pe.wait_ge(s.cx_h, 1)
        for b in range(16):
            bank_free(a)
            for i in range(2):
                g = 2 * b + i
                o = BANK[a % 4][:, i * CH:(i + 1) * CH]
                mm(o, LOC[:, g, :], U[:, g, :], start=True, stop=False, skip_group_check=True)
                mm(o, CA[:, g, :], H[:, 0, g, :], start=False, stop=False, skip_group_check=True)
                mm(o[:, 0:CL], CA[:, G + g, :], H[:, 1, g, CL - 1::-1], start=False, stop=True, skip_group_check=True)
                last = mm(o[:, CL:CH], CA[:, G + g, :], H[:, 1, g, CH - 1:CL - 1:-1], start=False, stop=True,
                          skip_group_check=True)
            last.then_inc(s.mm_act, 1)
            a += 1
        PE.transpose(BANK[6][0:Q, 0:P], FIN[:], ID[:]).then_inc(s.fin_mm, 1)
        pe.wait_ge(s.w_split, N_IN + 2)
        for g in range(NG):
            pe.wait_ge(s.y_split, g + 1)
            for m in range(4):
                bank_free(a)
                for k in range(4):
                    wh = WH[k // 2][:].rearrange("p (k f) -> p k f", k=2)[:, k % 2, m * P:(m + 1) * P]
                    wl = WL[k // 2][:].rearrange("p (k f) -> p k f", k=2)[:, k % 2, m * P:(m + 1) * P]
                    last = three(BANK[a % 4][:, 0:TG], (wh, wl), (YH[:, k, :], YL[:, k, :]), k == 0, k == 3)
                last.then_inc(s.mm_act, 1)
                a += 1
        def out_pair(b, t):
            for n in range(2):
                o_ = 18 * b + 2 * t + n
                if b == 0:
                    pe.wait_ge(s.mix_pool, t // 3 + 1)
                if b == 2:
                    pe.wait_ge(s.mix_ready, 4 * (t // 3 + 1))
                if o_ < 4:
                    pe.wait_ge(s.ev_act, A_STRAIGHT - 3 + o_)
                else:
                    pe.wait_ge(s.ev_dve, o_ - 3)
                for r in range(2):
                    k, w = 2 * b + r, w_slot(N_IN + N_GLU + 2 * b + r)
                    last = three(BANK[o_ % 4][:], (XH[:, k, t * P:(t + 1) * P], XL[:, k, t * P:(t + 1) * P]),
                                 (WH[w][:, n * 512:n * 512 + 512], WL[w][:, n * 512:n * 512 + 512]), r == 0, r == 1)
                last.then_inc(s.mm_dve, 1)
        for b in range(3):
            pe.wait_ge(s.w_split, N_IN + N_GLU + 2 * b + 2)
            for t in range(TT):
                out_pair(b, t)
        W1 = N_IN + N_GLU + N_OUT

        def hidden(ch, outs):
            for i in outs:
                g, m = i // 2, i % 2
                if i < 4:
                    pe.wait_ge(s.ev_dve, ch * 18 + (B_STRAIGHT - 3 + i))
                else:
                    pe.wait_ge(s.ev_act, ch * 6 + (A_STRAIGHT + i - 3))
                pe.wait_ge(s.h_lo, TT + 3 * (g + 1))
                for k in range(KB):
                    w = w_slot(W1 + k // 4)
                    wh = WH[w][:].rearrange("p (k f) -> p k f", k=4)[:, k % 4, m * P:(m + 1) * P]
                    wl = WL[w][:].rearrange("p (k f) -> p k f", k=4)[:, k % 4, m * P:(m + 1) * P]
                    last = three(BANK[i % 4][:, 0:TG], (wh, wl), (XH[:, k, g * TG:(g + 1) * TG], XL[:, k, g * TG:(g + 1) * TG]),
                                 k == 0, k == KB - 1)
                last.then_inc(s.mm_act, 1)

        def back(ch):
            pe.wait_ge(s.w_split, ch * 4 + (W1 + 4))
            for i in range(18):
                t, n = i // 2, i % 2
                pe.wait_ge(s.f_ready, ch * 6 + 2 * (t // 3 + 1))
                if i < 4:
                    pe.wait_ge(s.ev_act, ch * 6 + (A_STRAIGHT + 3 + i))
                else:
                    pe.wait_ge(s.ev_dve, ch * 18 + (B_STRAIGHT + i - 3))
                for r in range(2):
                    w = w_slot(W1 + 2 + r)
                    last = three(BANK[(6 + i) % 4][:], (FH[:, r, t * P:(t + 1) * P], FL[:, r, t * P:(t + 1) * P]),
                                 (WH[w][:, n * 512:n * 512 + 512], WL[w][:, n * 512:n * 512 + 512]), r == 0, r == 1)
                last.then_inc(s.mm_dve, 1)

        pe.wait_ge(s.w_split, N_IN + N_GLU + N_OUT)
        for t in range(TT):
            out_pair(3, t)
            if t >= LAG - 1:
                turn_tile(t - LAG + 1, XN[(t - LAG + 1) % 2], TT)
        pe.wait_ge(s.w_split, W1 + 2)
        for t in range(TT - LAG + 1, TT):
            hidden(0, [t - (TT - LAG + 1)])
            turn_tile(t, XN[t % 2], TT)
        hidden(0, range(LAG - 1, 6))
        back(0)
        with pe.Fori(1, NFC) as ch:
            pe.wait_ge(s.w_split, ch * 4 + (W1 + 2))
            hidden(ch, range(6))
            back(ch)

    block.__exit__(None, None, None)


_INS = ["x_prompt", "x_sample", "state_ssm", "c", "c_ctx", "norm_mix", "norm_mlp", "w_ada", "b_ada", "w_in", "w_out",
        "pool_w", "pool_scale", "ssm_a_re", "ssm_a_im", "ssm_log_dt", "ssm_b_re", "ssm_b_im", "ssm_c_re", "ssm_c_im",
        "ssm_d", "ssm_w_glu", "w_mlp1", "w_mlp2", "norm_out"]
_OUTS = [(1, CTX, D), (1, LAT, D), (1, 1, 2, G, N, 2)]


def _inverse_counts():
    import numpy as np

    def span(n, w):
        t = np.arange(n)
        return np.clip(t + w // 2, 0, n) - np.clip(t - w // 2, 0, n)

    out = np.empty((4, T), np.float32)
    for i in range(4):
        w = 2 << i
        out[i, :LAT] = (1.0 / np.outer(span(ROWS, w), span(GW, w))).ravel()
        out[i, LAT:] = 1.0 / span(CTX, w)
    return out


def kernel(**inputs):
    import numpy as np
    import concourse.bacc as bacc
    from concourse.bass_utils import run_bass_kernel_spmd

    nc = bacc.Bacc("TRN2", target_bir_lowering=False, num_devices=1)
    arrays = {f"in_{n}": np.ascontiguousarray(inputs[n]) for n in _INS}
    arrays["in_inv_count"] = _inverse_counts()
    args = [nc.dram_tensor(n, a.shape, mybir.dt.from_np(a.dtype), kind="ExternalInput").ap() for n, a in arrays.items()]
    outs = [nc.dram_tensor(f"out_{i}", shape, F32, kind="ExternalOutput").ap() for i, shape in enumerate(_OUTS)]
    build(nc, *args, *outs)
    r = run_bass_kernel_spmd(nc, [arrays], core_ids=[0])
    return tuple(r.results[0][f"out_{i}"] for i in range(len(_OUTS)))
```

```python
import concourse.bass as bass
from concourse import mybir

F32 = mybir.dt.float32
F32R = mybir.dt.float32r
ALU = mybir.AluOpType
ACT = mybir.ActivationFunctionType

P = 128
D = 1024
KB = D // P
LAT, CTX = 1024, 128
T = LAT + CTX
TT = T // P
TG = 384
NG = T // TG
L = 8
CL, CC = LAT // L, CTX // L
CH = CL + CC
G, N, SP = 32, 64, 16
Q = 2 * G
DFF = 4 * D
FC = 256
NFC = DFF // FC
ROWS, GW = 16, 64
EPS = 1e-6
MAGIC = 1.5 * 2.0 ** 23
TWO_PI = (6.28125, 1.93500518798828125e-3, 3.0199159819e-7)
PITCH = GW + 8
PADDED = 31 * PITCH + 8
CPAD = CTX + 16

KBYTE = 1024
RESERVED = 16 * KBYTE + 128


def build(nc, x_prompt, x_sample, state_ssm, c, c_ctx, norm_mix, norm_mlp, w_ada, b_ada, w_in, w_out, pool_w,
          pool_scale, ssm_a_re, ssm_a_im, ssm_log_dt, ssm_b_re, ssm_b_im, ssm_c_re, ssm_c_im, ssm_d,
          ssm_w_glu, w_mlp1, w_mlp2, norm_out, inv_count, y_prompt, y_sample, new_state):
    V, S, PE, GP = nc.vector, nc.scalar, nc.tensor, nc.gpsimd

    def at(name, shape, offset, dt=F32):
        return nc.alloc_sbuf_tensor_at(name, list(shape), dt, offset=offset)

    R_X, R_W, R_RAW, R_A, R_U, R_P, R_S, R_C = (RESERVED + k * 512 for k in (0, 144, 208, 240, 304, 340, 376, 395))
    XH = at("x_hi", [P, KB, T], R_X, F32R)
    XL = at("x_lo", [P, KB, T], R_X + 36 * KBYTE, F32R)
    WH = [at(f"w_hi{i}", [P, 1024], R_W + i * 8 * KBYTE, F32R) for i in range(4)]
    WL = [at(f"w_lo{i}", [P, 1024], R_W + i * 8 * KBYTE + 4 * KBYTE, F32R) for i in range(4)]
    RAW = [at(f"raw{i}", [P, 1024], R_RAW + i * 4 * KBYTE) for i in range(4)]
    XS = [at(f"x_tile{i}", [P, D], R_W + (16 + 4 * i) * KBYTE if i < 2 else R_A + 4 * (i - 1) * KBYTE) for i in range(TT)]
    B2 = at("b_bar_turned", [P, Q, SP], R_W + 24 * KBYTE)
    WB = at("to_state", [P, Q, P], R_A)
    SQ0 = at("square_dump0", [P, D], R_A)
    HT0 = [at(f"h_tile{i}", [P, KB, P], R_S + i * 4 * KBYTE) for i in range(2)]
    PROJ = [at(f"proj{i}", [P, T], R_U + 9 * KBYTE + i * 4608) for i in range(2)]
    POOL = at("pool_in", [P, 4, T], R_P)
    U = at("u_chunks", [P, G, CH], R_U)
    BX = at("b_re_im", [P, Q, SP], R_P)
    BY = at("b_im_re", [P, Q, SP], R_P + 4 * KBYTE)
    ROW0 = at("ada_row0", [2, 512], R_P + 8 * KBYTE)
    BIAS0 = at("ada_bias0", [1, 2048], R_P + 10 * KBYTE)
    small = [R_U]

    def tiny(name, shape):
        n = 4
        for x in shape[1:]:
            n *= x
        small[0] += (n + 31) // 32 * 32
        return at(name, shape, small[0] - (n + 31) // 32 * 32)

    VEC = tiny("vector_rows", [36, P])
    LDT = tiny("log_dt", [Q, 1])
    DT = tiny("dt", [Q, 1])
    AR, AI, EX, TH, KT, RT = (tiny(n, [Q, N]) for n in ("a_re", "a_im", "growth", "angle", "turns", "rest"))
    SR, SH, C0, NR, DEN, RD = (tiny(n, [Q, N]) for n in ("sine", "half_sine", "cosine", "nom", "den", "rden"))
    M1, M2, M3, M4 = (tiny(f"m{i}", [Q, N]) for i in range(4))
    TAB = tiny("tables", [Q, 4, P])
    ZR, ZS, ZT, ZU = (tiny(n, [P, Q]) for n in ("z_re", "z_im_signed", "z_re_signed", "z_im_neg"))
    ZI = tiny("z_im", [P, Q])
    SGN = tiny("sign", [P, 1])
    TB = tiny("b_tmp", [P, Q, SP])
    TW = [tiny(f"to_state_tmp{i}", [P, G, SP]) for i in range(2)]
    PT = [tiny(f"pow_tmp{i}", [P, 4, Q]) for i in range(2)]
    assert small[0] <= R_P
    B1 = at("b_bar", [P, Q, SP], R_C)
    PR = at("pow_re", [P, L + 1, Q], R_C + 4096)
    PI = at("pow_im", [P, L + 1, Q], R_C + 6400)
    ID = at("identity", [P, P], R_C + 8704)
    AQ = at("a8_im_signed", [P, Q], R_C + 9216)
    FIN = at("ctx_final", [P, Q], R_C + 9472)
    ADA = [at(f"ada_cols{i}", [P, 2, KB], R_C + 9728 + 64 * i) for i in range(4)]
    COL = at("vector_cols", [P, 36], R_C + 9984)
    EPSB = at("eps", [P, 1], R_C + 10144)
    CSG = at("c_sign", [P, 1], R_C + 10176)
    ONE = at("ones", [1, 2], R_C + 10208)
    STAT = [at(f"stat{i}", [P, TT], R_C + 10240 + 64 * i) for i in range(3)]
    H = at("states", [P, 2, G, CH], R_X)
    CA = at("from_state", [P, Q, P], R_X + 36 * KBYTE)
    ROW2 = at("ada_row2", [2, 512], R_X + 68 * KBYTE)
    BIAS2 = [at(f"ada_bias2_{i}", [1, 512], o) for i, o in enumerate((R_X + 70 * KBYTE, R_A, R_A + 30 * KBYTE))]
    C1 = at("c_signed", [P, Q, SP], R_W)
    C2 = at("c_turned", [P, Q, SP], R_W + 4 * KBYTE)
    PAD = [at(f"padded{i}", [P, PADDED + CPAD], o) for i, o in enumerate((R_W + 16 * KBYTE, R_S))]
    TP, TQ = (at(f"pair_{n}", [P, 2, 8, CH // 2], R_S + k * 4608) for k, n in enumerate("pq"))
    LOC = at("local", [P, G, P], R_W + 8 * KBYTE)
    o = R_W + 8 * KBYTE + 2 * 9536
    PS_, QS_, RS_ = (at(f"step_{n}", [P, 2, Q], o + 512 * k) for k, n in enumerate("pqr"))
    A2R, A2I = (at(f"a16_{n}", [P, Q], o + 4608 + 256 * k) for k, n in enumerate(("re", "im_signed")))
    DD = at("d_diag", [SP, G, SP], o + 1536)
    ST = at("state_rows", [Q, N, 2], o + 1536 + 2048)
    STR = at("state_rows_split", [Q, 2, N], o + 1536 + 2560)
    KK = at("kernels", [SP, G, 15, SP], R_A)
    CT = at("ca_tmp", [P, G, SP], R_A + 30 * KBYTE)
    CS = at("c_rows", [P, 8, 3, N], R_X + 36 * KBYTE)
    PWS = at("pool_w_sb", [P, 4, P], R_W + 24 * KBYTE)
    INV = at("inv_count_b", [P, T], R_W + 16 * KBYTE + 9536)
    Y = at("y_chunks", [P, G, CH], R_U)
    ACC = at("acc", [P, TT, D], R_A)
    o3 = R_A + 36 * KBYTE
    YR = at("y_rows", [P, 4, T], o3)
    YH = at("y_hi", [P, 4, TG], o3 + 18 * KBYTE, F32R)
    YL = at("y_lo", [P, 4, TG], o3 + 24 * KBYTE, F32R)
    STO = at("state_out", [Q, N, 2], R_S + 9216)
    SZ = [at(f"sigmoid{i}", [P, TG], o3 + 30 * KBYTE + 1536 * i) for i in range(2)]
    SO = at("ssm_out", [P, TG], o3 + 33 * KBYTE)
    GB = at("gate_b", [P, 2, D], R_C)
    FH = at("f_hi", [P, 2, T], o3, F32R)
    FL = at("f_lo", [P, 2, T], o3 + 9 * KBYTE, F32R)
    RL = [at(f"relu{i}", [P, TG], o3 + 18 * KBYTE + 1536 * i) for i in range(2)]
    FT = [at(f"f_tmp{i}", [P, TG], o3 + 21 * KBYTE + 1536 * i) for i in range(2)]
    BT = [at(f"gated{i}", [P, 512], o3 + 24 * KBYTE + 2048 * i) for i in range(4)]
    HT1 = [at(f"h1_tile{i}", [P, KB, P], o3 + 24 * KBYTE + i * 4 * KBYTE) for i in range(2)]
    XN = [at(f"xn_tile{i}", [P, D], o3 + i * 4 * KBYTE) for i in range(2)]
    NO = at("norm_out_b", [P, D], o3 + 32 * KBYTE)
    SQ = at("square_dump", [P, D], o3 + 36 * KBYTE)
    SQ1 = at("square_dump1", [P, D], o3 + 8 * KBYTE)
    BT3 = [at(f"gated3_{i}", [P, 512], R_S + 3072 + 2048 * i) for i in range(3)]

    BANK = [nc.alloc_psum_tensor(f"bank{i}", [P, 512], F32) for i in range(8)]

    def scratch(name, shape):
        return nc.dram_tensor(name, shape, F32, kind="Internal").ap()

    UD, YD = scratch("u_rows", (512, T)), scratch("ssm_rows", (512, T))
    GD = scratch("gates", (2, 2, D))

    names = ["raw0", "raw1", "raw2", "raw3", "ada_used", "w_hi", "w_split", "mm_act", "mm_dve", "ev_act",
             "ev_dve", "vec_in", "dtab_in", "b_in", "bias0_in", "xt0", "xt1", "xt2", "xt3", "xt4", "xt5", "xt6", "xt7", "xt8", "id_ready", "id_zero", "sgn_ready",
             "dve", "pe_small", "col_ready", "silu_done", "ada_mm", "row_ready", "ada_cols",
             "tab_dt", "tab_e", "tab_th", "tab_sin", "wbt", "wbt_mm", "wb_ready", "sq", "root", "xn", "tr", "aff_d", "aff_a",
             "h_hi", "h_lo", "ud_w0", "ud_w1", "ud_w2", "ud_w3", "u_in0", "u_in1", "st_in",
             "cs_in", "inv_in", "dd_in", "dd_ready", "c_mm", "c_ready", "h0_mm", "h_init", "pad_zero", "pooled",
             "ca", "ca_ready", "sc_p", "sc_r", "sc_h", "cx_h", "gates_w", "bias_even_in", "bias_odd_in", "pw_in",
             "kk_mm", "kk_ready", "loc_in", "yd_w", "yr0", "yr1", "yr2", 
             "y_split_hi", "y_split", "so", "mix_hi", "mix_pool", "mix_ready", "gb_in",
             "acc_in", "acc_ctx_in", "acc", "filled", "f_ready", "fin_mm", "fin_ready", "fin_out", "no_in", "y_final",
             "out_w", "acts", "tabs", "ada0", "sqr"]
    sem = {n: nc.alloc_semaphore(n) for n in names}
    s = type("Sems", (), sem)
    x_in = [s.xt0, s.xt1, s.xt2, s.xt3, s.xt4, s.xt5, s.xt6, s.xt7, s.xt8]

    N_ADA0, N_IN, N_ADA2, N_GLU, N_OUT = 16, 8, 32, 2, 8
    FIRST_IN = N_ADA0
    FIRST_ADA2 = FIRST_IN + N_IN
    FIRST_GLU = FIRST_ADA2 + N_ADA2
    FIRST_OUT = FIRST_GLU + N_GLU
    FIRST_MLP = FIRST_OUT + N_OUT
    raw_in = [s.raw0, s.raw1, s.raw2, s.raw3]
    PARTS = [1, 0, 2, 3, 4, 5]

    def raw_landed(eng, n):
        eng.wait_ge(raw_in[n % 4], 16 * (n // 4 + 1))

    def w_slot(w):
        if w < N_IN:
            return w % 2
        return (0, 3, 1, 2)[(w - N_IN) % 4]

    ada_v = w_ada[0].rearrange("(k p) n -> p k n", p=P)
    in_v = w_in[0].rearrange("(k p) n -> p k n", p=P)
    glu_v = ssm_w_glu[0].rearrange("(k p) n -> p k n", p=P)
    w1_v = w_mlp1[0].rearrange("(k p) n -> p k n", p=P)
    xs_v = x_sample[0].rearrange("(c j) d -> c j d", j=L)
    xp_v = x_prompt[0].rearrange("(c j) d -> j c d", j=L)
    ys_v = y_sample[0].rearrange("(c j) d -> c j d", j=L)
    yp_v = y_prompt[0].rearrange("(c j) d -> j c d", j=L)

    IN_END = NG * KB
    S_END = IN_END + Q // 2
    MAPS_END = S_END + 4 * NG
    Y_END = MAPS_END + G // 2
    A_STRAIGHT = Y_END + 4 * NG
    B_STRAIGHT = 4 * 18
    def y_split(g):
        if g == NG - 1:
            return YH[:], YL[:]
        cols = slice((g + 1) * TG, (g + 2) * TG)
        return XH[:, 4:KB, cols], XL[:, 4:KB, cols]

    def bias_row(k):
        return BIAS2[0 if k % 2 == 0 else 1 if k < 7 else 2]

    def turn_banks(t, odd):
        return (BANK[4], BANK[5]) if t % 2 == 0 else (BANK[odd], BANK[odd + 1])

    LAG = 3

    def grid(buf, r0, r1, shift=0):
        o = (r0 + 8) * PITCH + 8
        return buf[:, o:o + (r1 - r0) * PITCH].rearrange("p (r c) -> p r c", c=PITCH)[:, :, shift:shift + GW]

    def ctx(buf, lo, hi):
        return buf[:, PADDED + 8 + lo:PADDED + 8 + hi]

    def pool_window(dve, tt, then, copy, gi):
        w = 2 << gi
        dve.wait_ge(s.pad_zero, 2 * gi + 2)
        dve.wait_ge(s.ev_act, 3 * gi + 3)
        a_, b_ = PAD
        lat_in = POOL[:, gi, 0:LAT].rearrange("p (r c) -> p r c", c=GW)
        then(copy(grid(a_, 0, ROWS), lat_in))
        then(copy(ctx(a_, 0, CTX), POOL[:, gi, LAT:T]))
        first, last = 8 * PITCH + 8, (8 + ROWS - 1) * PITCH + 8 + GW
        for st in range(gi + 1):
            back, ahead = (1, 0) if st == 0 else (1 << (st - 1), 1 << (st - 1))
            ext = w // 2 - (1 << st)
            lo, hi = first - ext, last + ext
            then(tt(b_[:, lo:hi], a_[:, lo - back:hi - back], a_[:, lo + ahead:hi + ahead], ALU.add))
            then(tt(ctx(b_, -ext, CTX + ext), ctx(a_, -ext - back, CTX + ext - back),
                    ctx(a_, -ext + ahead, CTX + ext + ahead), ALU.add))
            a_, b_ = b_, a_
        sums = a_
        for st in range(gi + 1):
            back, ahead = (1, 0) if st == 0 else (1 << (st - 1), 1 << (st - 1))
            ext = w // 2 - (1 << st)
            then(tt(grid(b_, -ext, ROWS + ext), grid(a_, -ext - back, ROWS + ext - back),
                    grid(a_, -ext + ahead, ROWS + ext + ahead), ALU.add))
            a_, b_ = b_, a_
        dve.wait_ge(s.inv_in, 16 * (gi + 1))
        then(tt(grid(a_, 0, ROWS), grid(a_, 0, ROWS), INV[:, 0:LAT].rearrange("p (r c) -> p r c", c=GW), ALU.mult))
        then(tt(ctx(sums, 0, CTX), ctx(sums, 0, CTX), INV[:, LAT:T], ALU.mult))
        then(tt(lat_in, grid(a_, 0, ROWS), lat_in, ALU.subtract))
        tt(POOL[:, gi, LAT:T], ctx(sums, 0, CTX), POOL[:, gi, LAT:T], ALU.subtract).then_inc(s.pooled, 1)
        dve.wait_ge(s.pooled, gi + 1)

    block = nc.Block()
    block.__enter__()

    def lat_j3(ap):
        return ap.rearrange("p (j c) -> p j c", c=CL)

    uds = [s.ud_w0, s.ud_w1, s.ud_w2, s.ud_w3]

    @block.sync
    def _(sp):
        def free(n):
            m = n - 4
            if m < 0:
                return
            if m < FIRST_IN:
                sp.wait_ge(s.ada_used, m + 1)
            elif m < FIRST_ADA2:
                sp.wait_ge(s.w_split, m - FIRST_IN + 1)
            elif m < FIRST_GLU:
                sp.wait_ge(s.ada_used, N_ADA0 + m - FIRST_ADA2 + 1)
            else:
                sp.wait_ge(s.w_split, N_IN + m - FIRST_GLU + 1)

        def load(n, dst, src):
            free(n)
            sp.dma_start(dst, src).then_inc(raw_in[n % 4], 16)

        def load_ada(n, i):
            part, k = PARTS[i // KB], i % KB
            load(n, RAW[n % 4][:], ada_v[:, k, part * D:(part + 1) * D])

        for i, (v, n) in enumerate(((c[0], 8), (c_ctx, 8), (norm_mix[0], 8), (norm_mlp[0], 8), (pool_scale[0], 4))):
            sp.dma_start(VEC[8 * i:8 * i + n, :], v.rearrange("(k p) -> k p", p=P)).then_inc(s.vec_in, 16)
        for i in range(N_ADA0):
            load_ada(i, i)
        for i in range(N_IN):
            n = FIRST_IN + i
            load(n, RAW[n % 4][:].rearrange("p (k f) -> p k f", k=KB), in_v[:, :, i * P:(i + 1) * P])
        sp.wait_ge(s.wbt, 2 * L)
        sp.dma_start(ST[:].rearrange("q n r -> q (n r)"), state_ssm[0, 0].rearrange("d g n r -> (d g) (n r)")).then_inc(s.st_in, 16)
        for i in range(4):
            load_ada(FIRST_ADA2 + i, N_ADA0 + i)
        for half in range(2):
            sp.wait_ge(uds[2 * half], 16)
            sp.wait_ge(uds[2 * half + 1], 16)
            g0 = 16 * half
            ud = UD[g0 * SP:(g0 + 16) * SP, :].rearrange("(g p) t -> p g t", p=SP)
            for j in range(L):
                dst = U[j * SP:(j + 1) * SP, g0:g0 + 16, :]
                sp.dma_start(dst[:, :, 0:CL], ud[:, :, j * CL:(j + 1) * CL]).then_inc(s.u_in0 if half == 0 else s.u_in1, 16)
                sp.dma_start(dst[:, :, CL:CH], ud[:, :, LAT + j * CC:LAT + (j + 1) * CC])\
                  .then_inc(s.u_in0 if half == 0 else s.u_in1, 16)
        sp.wait_ge(s.mm_act, IN_END)
        for k, src in enumerate((ssm_c_re, ssm_c_im, ssm_c_re)):
            sp.dma_start(CS[:, :, k, :], src[0].rearrange("d (b g) p n -> (g p) (d b) n", g=8)).then_inc(s.cs_in, 16)
        sp.wait_ge(s.pooled, 4)
        sp.dma_start(DD[:].rearrange("p g c -> p (g c)"), ssm_d[0].rearrange("g p -> (g p)").partition_broadcast(SP)).then_inc(s.dd_in, 16)
        for i in range(4, N_ADA2):
            load_ada(FIRST_ADA2 + i, N_ADA0 + i)
        for i in range(2):
            n = FIRST_GLU + i
            load(n, RAW[n % 4][:], w_out[0, i * P:(i + 1) * P, :])
        for i in range(N_GLU):
            n = FIRST_GLU + 2 + i
            load(n, RAW[n % 4][:].rearrange("p (k f) -> p k f", k=2), glu_v[:, 2 * i:2 * i + 2, :])
        sp.wait_ge(s.loc_in, 16 * L)
        sp.wait_ge(s.ca_ready, 2 * L)
        sp.wait_ge(s.gb_in, 16)
        sp.dma_start(ACC[:, 0:L, :], xs_v).then_inc(s.acc_in, 16)
        sp.wait_ge(s.ev_act, Y_END)
        yd = YD.rearrange("(g p) t -> p g t", p=SP)
        for j in range(L):
            src = Y[j * SP:(j + 1) * SP, :, :]
            sp.dma_start(yd[:, :, j * CL:(j + 1) * CL], src[:, :, 0:CL]).then_inc(s.yd_w, 16)
            sp.dma_start(yd[:, :, LAT + j * CC:LAT + (j + 1) * CC], src[:, :, CL:CH]).then_inc(s.yd_w, 16)
        sp.wait_ge(s.yd_w, 16 * 16)
        sp.wait_ge(s.mix_pool, NG)
        yds = YD.rearrange("(k p) t -> p k t", p=P)
        for g, q in enumerate((s.yr0, s.yr1, s.yr2)):
            sp.dma_start(YR[:, :, g * TG:(g + 1) * TG], yds[:, :, g * TG:(g + 1) * TG]).then_inc(q, 16)
        for j in range(L):
            sp.dma_start(ACC[j * CC:(j + 1) * CC, L, :], xp_v[j]).then_inc(s.acc_ctx_in, 16)
        sp.wait_ge(s.fin_ready, 1)
        sp.dma_start(new_state[0, 0].rearrange("d g n r -> (d g) (n r)"), STO[:].rearrange("q n r -> q (n r)")).then_inc(s.fin_out, 16)
        for i in range(2, N_OUT):
            n = FIRST_OUT + i
            load(n, RAW[n % 4][:], w_out[0, i * P:(i + 1) * P, :])
        with sp.Fori(0, NFC) as ch:
            for i in range(4):
                n = FIRST_MLP + i
                sp.wait_ge(s.w_split, ch * 4 + (N_IN + n - 4 - FIRST_GLU + 1))
                if i < 2:
                    dst, src = RAW[n % 4][:].rearrange("p (k f) -> p k f", k=4), w1_v[:, 4 * i:4 * i + 4, bass.ds(ch * FC, FC)]
                else:
                    dst, src = RAW[n % 4][:], w_mlp2[0, bass.ds(ch * FC + (i - 2) * P, P), :]
                sp.dma_start(dst, src).then_inc(raw_in[n % 4], 16)
        for t in range(TT):
            sp.wait_ge(s.y_final, t + 1)
            if t < L:
                sp.dma_start(ys_v[:, t, :], ACC[:, t, :]).then_inc(s.out_w, 16)
            else:
                for j in range(L):
                    sp.dma_start(yp_v[j], ACC[j * CC:(j + 1) * CC, t, :]).then_inc(s.out_w, 16)
        sp.wait_ge(s.out_w, 16 * (2 * L))
        sp.wait_ge(s.fin_out, 16)

    @block.gpsimd
    def _(gp):
        GP.memset(ID[:], 0.0).then_inc(s.id_zero, 1)
        gp.wait_ge(s.id_zero, 1)
        GP.affine_select(out=ID[:], in_=ID[:], compare_op=ALU.not_equal, fill=1.0, base=0, pattern=[[-1, P]],
                         channel_multiplier=1).then_inc(s.id_ready, 1)
        gp.wait_ge(s.id_ready, 1)
        GP.memset(SGN[0:N, :], -1.0).then_inc(s.sgn_ready, 1)
        gp.wait_ge(s.sgn_ready, 1)
        GP.memset(SGN[N:P, :], 1.0).then_inc(s.sgn_ready, 1)
        gp.wait_ge(s.sgn_ready, 2)
        GP.memset(ONE[:], 1.0).then_inc(s.sgn_ready, 1)
        for t in range(TT):
            if t:
                gp.wait_ge(s.ada_used, t)
            if t < L:
                gp.dma_start(XS[t][:], xs_v[:, t, :]).then_inc(x_in[t], 16)
            else:
                for j in range(L):
                    gp.dma_start(XS[t][j * CC:(j + 1) * CC, :], xp_v[j]).then_inc(x_in[t], 16)
        def window_setup(gi):
            if gi:
                gp.wait_ge(s.pooled, gi)
            for i in range(2):
                GP.memset(PAD[i][:], 0.0).then_inc(s.pad_zero, 1)
                gp.wait_ge(s.pad_zero, 2 * gi + i + 1)
            gp.dma_start(INV[:], inv_count[gi].partition_broadcast(P)).then_inc(s.inv_in, 16)

        gp.wait_ge(s.wbt, 2 * L)
        for gi in range(4):
            window_setup(gi)
        gp.wait_ge(s.pooled, 4)
        gp.dma_start(PWS[:], pool_w[0].rearrange("i c d -> c i d")).then_inc(s.pw_in, 16)
        gp.wait_ge(s.mm_act, S_END)
        gp.wait_ge(s.c_ready, 16)
        n = 0
        for d in range(2):
            for j in range(L):
                e = j + 1 if d == 0 else L - j
                q0 = d * G
                out = CA[:, q0:q0 + G, j * SP:(j + 1) * SP]
                pr = PR[:, e, q0:q0 + G].unsqueeze(2).to_broadcast([P, G, SP])
                pi = PI[:, e, q0:q0 + G].unsqueeze(2).to_broadcast([P, G, SP])
                if n:
                    gp.wait_ge(s.ca_ready, n)
                GP.tensor_tensor(out, C1[:, q0:q0 + G, :], pr, ALU.mult).then_inc(s.ca, 1)
                gp.wait_ge(s.ca, 2 * n + 1)
                GP.tensor_tensor(CT[:], C2[:, q0:q0 + G, :], pi, ALU.mult).then_inc(s.ca, 1)
                n += 1
                gp.wait_ge(s.ca, 2 * n)
                GP.tensor_tensor(out, out, CT[:], ALU.add).then_inc(s.ca_ready, 1)
        gp.wait_ge(s.ca_ready, 2 * L)
        gp.wait_ge(s.dd_in, 16)
        GP.tensor_tensor(DD[:], DD[:], ID[0:SP, 0:SP].unsqueeze(1).to_broadcast([SP, G, SP]), ALU.mult).then_inc(s.dd_ready, 1)
        gp.wait_ge(s.kk_ready, 16)
        kv = KK[:].rearrange("p g e c -> p g (e c)")
        for j in range(L):
            gp.dma_start(LOC[j * SP:(j + 1) * SP, :, :], kv[:, :, (L - 1 - j) * SP:(L - 1 - j) * SP + P]).then_inc(s.loc_in, 16)
        gp.wait_ge(s.gates_w, 16 * 2 * 2)
        gp.wait_ge(s.cx_h, 1)
        gp.dma_start(GB[:].rearrange("p a d -> p (a d)"), GD[0].rearrange("a d -> (a d)").partition_broadcast(P)).then_inc(s.gb_in, 16)
        gp.wait_ge(s.acc_in, 16)
        for i in range(B_STRAIGHT):
            o_ = i % 18
            gp.wait_ge(s.ev_dve, i + 1)
            a = ACC[:, o_ // 2, (o_ % 2) * 512:(o_ % 2) * 512 + 512]
            if i:
                gp.wait_ge(s.acc, i)
            if i == 2 * L:
                gp.wait_ge(s.acc_ctx_in, 16 * L)
            GP.tensor_tensor(a, a, BT3[i % 3][:], ALU.add).then_inc(s.acc, 1)
        gp.wait_ge(s.ev_dve, B_STRAIGHT)
        gp.dma_start(GB[:].rearrange("p a d -> p (a d)"), GD[1].rearrange("a d -> (a d)").partition_broadcast(P)).then_inc(s.gb_in, 16)
        gp.wait_ge(s.tr, 2 * TT)
        gp.dma_start(NO[:], norm_out.partition_broadcast(P)).then_inc(s.no_in, 16)
        with gp.Fori(0, NFC) as ch:
            for i in range(18):
                gp.wait_ge(s.ev_dve, ch * 18 + (B_STRAIGHT + i + 1))
                gp.wait_ge(s.acc, ch * 18 + (B_STRAIGHT + i))
                a = ACC[:, i // 2, (i % 2) * 512:(i % 2) * 512 + 512]
                GP.tensor_tensor(a, a, BT[i % 4][:], ALU.add).then_inc(s.acc, 1)

    @block.scalar
    def _(act):
        act.dma_start(LDT[:], ssm_log_dt[0].rearrange("d g -> (d g)").unsqueeze(1)).then_inc(s.dtab_in, 16)
        act.dma_start(AR[:], ssm_a_re[0].rearrange("d g n -> (d g) n")).then_inc(s.dtab_in, 16)
        act.dma_start(AI[:], ssm_a_im[0].rearrange("d g n -> (d g) n")).then_inc(s.dtab_in, 16)
        for k in range(2):
            part = PARTS[k]
            act.dma_start(BIAS0[:, k * D:(k + 1) * D], b_ada[:, part * D:(part + 1) * D]).then_inc(s.bias0_in, 16)
        for dst, top, bot in ((BX, ssm_b_re, ssm_b_im), (BY, ssm_b_im, ssm_b_re)):
            act.dma_start(dst[0:N], top[0].rearrange("d g n p -> n (d g) p")).then_inc(s.b_in, 16)
            act.dma_start(dst[N:P], bot[0].rearrange("d g n p -> n (d g) p")).then_inc(s.b_in, 16)
        act.wait_ge(s.col_ready, 1)
        S.activation(COL[:, 0:16], COL[:, 0:16], ACT.Silu).then_inc(s.silu_done, 1)
        act.wait_ge(s.dtab_in, 48)
        S.activation(DT[:], LDT[:], ACT.Exp).then_inc(s.tab_dt, 1)
        act.wait_ge(s.tab_th, 1)
        S.activation(EX[:], M1[:], ACT.Exp).then_inc(s.tab_e, 1)
        act.wait_ge(s.tab_th, 2)
        S.activation(SR[:], RT[:], ACT.Sin).then_inc(s.tab_sin, 1)
        S.activation(SH[:], RT[:], ACT.Sin, scale=0.5).then_inc(s.tab_sin, 1)

        def stats(t, src, dump, base):
            S.activation(dump, src, ACT.Square, accum_out=STAT[0][:, t:t + 1]).then_inc(s.sq, 1)
            act.wait_ge(s.sq, base + t + 1)
            S.activation(STAT[1][:, t:t + 1], STAT[0][:, t:t + 1], ACT.Sqrt, bias=EPSB[:], scale=1.0 / D).then_inc(s.root, 1)

        def affine(t, ht, ada, base):
            cond = 0 if t < L else 1
            act.wait_ge(s.tr, base + t + 1)
            if base + t >= 2:
                act.wait_ge(s.h_lo, base + t - 1)
            for k in range(4, KB):
                S.activation(ht[t % 2][:, k, :], turn_banks(t, 6 if base else 2)[1][:, (k - 4) * P:(k - 3) * P], ACT.Identity,
                             scale=ADA[ada][:, cond, k:k + 1], bias=ADA[ada + 1][:, cond, k:k + 1]).then_inc(s.aff_a, 1)

        def round_hi(t, ht, base):
            act.wait_ge(s.aff_a, 4 * (base + t + 1))
            act.wait_ge(s.aff_d, 4 * (base + t + 1))
            S.activation(XH[:, :, t * P:(t + 1) * P], ht[t % 2][:], ACT.Copy).then_inc(s.h_hi, 1)

        def split_hi(w, n):
            raw_landed(act, n)
            if w < N_IN:
                if w >= 2:
                    act.wait_ge(s.mm_act, 3 * (w - 1))
            elif w == N_IN:
                act.wait_ge(s.mm_act, MAPS_END)
            elif w == N_IN + 1:
                act.wait_ge(s.cx_h, 1)
            elif w < N_IN + 4:
                act.wait_ge(s.mm_act, Y_END)
            elif w in (N_IN + 6, N_IN + 7):
                act.wait_ge(s.mm_act, A_STRAIGHT)
            else:
                act.wait_ge(s.mm_dve, 18 * max((w - N_IN - 4) // 2, 1))
            S.activation(WH[w_slot(w)][:], RAW[n % 4][:], ACT.Copy).then_inc(s.w_hi, 1)

        act.wait_ge(s.tabs, 2)
        for t in range(TT):
            act.wait_ge(x_in[t], 16 if t < L else 16 * L)
            stats(t, XS[t][:], SQ0[:], 0)
        n_row = 0
        for part in range(2):
            for hf in range(2):
                act.wait_ge(s.ada_mm, part + 1)
                if n_row:
                    act.wait_ge(s.ada_cols, n_row)
                S.activation(ROW0[:], BANK[2 * part + hf][0:2, :], ACT.Copy).then_inc(s.row_ready, 1)
                n_row += 1
        act.wait_ge(s.ada0, 2)
        affine(0, HT0, 0, 0)
        for t in range(TT):
            if t + 1 < TT:
                affine(t + 1, HT0, 0, 0)
            round_hi(t, HT0, 0)
            if t < 2:
                split_hi(t, FIRST_IN + t)
        uds = [s.ud_w0, s.ud_w1, s.ud_w2, s.ud_w3]
        a = 0
        for mb in range(KB):
            for g in range(NG):
                act.wait_ge(s.mm_act, a + 1)
                src = BANK[a % 4][:, 0:TG]
                if mb < 4:
                    if a == 0:
                        act.wait_ge(s.tabs, 4)
                    dst = POOL[:, mb, :]
                    dl = dst[:, 0:LAT].rearrange("p (c j) -> p j c", j=L)
                    if g < 2:
                        S.activation(dl[:, 3 * g:3 * g + 3, :], src.rearrange("p (j c) -> p j c", c=CL), ACT.Copy).then_inc(s.ev_act, 1)
                    else:
                        S.activation(dl[:, 6:8, :], src[:, 0:256].rearrange("p (j c) -> p j c", c=CL), ACT.Copy).then_inc(s.acts, 1)
                        S.activation(dst[:, LAT:T].rearrange("p (c j) -> p j c", j=L),
                                     src[:, 256:384].rearrange("p (j c) -> p j c", c=CC), ACT.Copy).then_inc(s.ev_act, 1)
                else:
                    if mb >= 6:
                        act.wait_ge(uds[mb - 6], 16)
                    if a == 12:
                        act.wait_ge(s.wbt, 2 * L)
                    S.activation(PROJ[mb % 2][:, g * TG:(g + 1) * TG], src, ACT.Copy).then_inc(s.ev_act, 1)
                a += 1
            if mb >= 4:
                act.wait_ge(s.ev_act, a)
                act.dma_start(UD[(mb - 4) * P:(mb - 3) * P, :], PROJ[mb % 2][:]).then_inc(uds[mb - 4], 16)
            if mb == 4:
                for b in range(16):
                    act.wait_ge(s.wbt_mm, b + 1)
                    S.activation(WB[:, 4 * b:4 * b + 4, :].rearrange("p q c -> p (q c)"), BANK[6 + b % 2][:], ACT.Copy)\
                     .then_inc(s.wb_ready, 1)
            if mb + 2 < KB:
                split_hi(mb + 2, FIRST_IN + mb + 2)
        act.wait_ge(s.mm_act, IN_END)
        for b in range(32):
            g0, d = 2 * (b // 2), b % 2
            act.wait_ge(s.mm_act, a + 1)
            src = BANK[a % 4][:, 0:2 * CH].rearrange("p (g c) -> p g c", g=2)
            hs = H[:, d, g0:g0 + 2, :]
            fin = FIN[:, d * G + g0:d * G + g0 + 2].unsqueeze(2)
            if d == 0:
                S.activation(hs[:, :, 1:CL], src[:, :, 0:CL - 1], ACT.Copy).then_inc(s.acts, 1)
                S.activation(hs[:, :, CL + 1:CH], src[:, :, CL:CH - 1], ACT.Copy).then_inc(s.acts, 1)
                S.activation(fin, src[:, :, CH - 1:CH], ACT.Copy).then_inc(s.ev_act, 1)
            else:
                S.activation(hs[:, :, CL - 1:0:-1], src[:, :, 1:CL], ACT.Copy).then_inc(s.acts, 1)
                S.activation(hs[:, :, CH - 1:CL:-1], src[:, :, CL + 1:CH], ACT.Copy).then_inc(s.acts, 1)
                S.activation(fin, src[:, :, CL:CL + 1], ACT.Copy).then_inc(s.ev_act, 1)
            a += 1
        for b in range(8):
            act.wait_ge(s.c_mm, b + 1)
            src = BANK[6 + b % 2]
            S.activation(C1[:, 8 * b:8 * b + 8, :].rearrange("p q c -> p (q c)"), src[:, 0:P], ACT.Copy, scale=CSG[:])\
             .then_inc(s.c_ready, 1)
            S.activation(C2[:, 8 * b:8 * b + 8, :].rearrange("p q c -> p (q c)"), src[:, P:2 * P], ACT.Copy, scale=-1.0)\
             .then_inc(s.c_ready, 1)
        def load_bias(k):
            if k == 7:
                act.wait_ge(s.ca_ready, 2 * L)
            act.dma_start(bias_row(k)[:], b_ada[:, 2 * D + 512 * k:2 * D + 512 * (k + 1)])\
               .then_inc(s.bias_odd_in if k % 2 else s.bias_even_in, 16)

        for k in range(2):
            load_bias(k)
        def ada_row(k):
            part, hf = k // 2, k % 2
            act.wait_ge(s.ada_mm, 3 + k)
            if k + 2 < 8:
                load_bias(k + 2)
            if k in (1, 2, 7):
                act.wait_ge(s.gates_w, {1: 16, 2: 32, 7: 48}[k])
            S.activation(ROW2[:], BANK[4 + k % 2][0:2, :], ACT.Copy).then_inc(s.row_ready, 1)
            if part in (0, 3):
                act.wait_ge(s.row_ready, 5 + k)
                act.dma_start(GD[part // 3, :, hf * 512:hf * 512 + 512], ROW2[:]).then_inc(s.gates_w, 16)
            else:
                act.wait_ge(s.ada_cols, 3 + k)
                cols = BANK[7][:, 64 + 8 * (k % 4):72 + 8 * (k % 4)].rearrange("p (k a) -> p a k", a=2)
                dst = ADA[3 if part == 1 else 2][:, :, 4 * hf:4 * hf + 4]
                S.activation(dst, cols, ACT.Copy).then_inc(s.acts, 1)
        for k in range(6):
            ada_row(k)
        for b in range(16):
            act.wait_ge(s.kk_mm, b + 1)
            S.activation(KK[:, 2 * b:2 * b + 2].rearrange("p g e c -> p (g e c)"), BANK[6 + b % 2][0:SP, 0:480], ACT.Copy)\
             .then_inc(s.kk_ready, 1)
        for k in range(6, 8):
            ada_row(k)
        for gi in range(4):
            act.wait_ge(s.mm_act, a + NG)
            for g in range(NG):
                S.activation(POOL[:, gi, g * TG:(g + 1) * TG], BANK[a % 4][:, 0:TG], ACT.Copy, scale=COL[:, 32 + gi:33 + gi])\
                 .then_inc(s.ev_act, 1)
                a += 1
        for w in range(2):
            split_hi(N_IN + w, FIRST_GLU + w)
        for b in range(16):
            act.wait_ge(s.mm_act, a + 1)
            S.activation(Y[:, 2 * b:2 * b + 2, :].rearrange("p g c -> p (g c)"), BANK[a % 4][:, 0:2 * CH], ACT.Gelu_apprx_tanh)\
             .then_inc(s.ev_act, 1)
            a += 1
        act.wait_ge(s.mm_act, Y_END)
        for g in range(NG):
            S.activation(XH[:, 0:4, g * TG:(g + 1) * TG], POOL[:, :, g * TG:(g + 1) * TG], ACT.Copy).then_inc(s.mix_hi, 1)
        for w in range(2, 4):
            split_hi(N_IN + w, FIRST_GLU + w)
        for g, q in enumerate((s.yr0, s.yr1, s.yr2)):
            act.wait_ge(q, 16)
            S.activation(y_split(g)[0], YR[:, :, g * TG:(g + 1) * TG], ACT.Copy).then_inc(s.y_split_hi, 1)
        for w in range(4, 6):
            split_hi(N_IN + w, FIRST_GLU + w)
        for g in range(NG):
            for m in range(4):
                act.wait_ge(s.mm_act, a + 1)
                if a - Y_END >= 2:
                    act.wait_ge(s.so, a - Y_END - 1)
                S.activation(SZ[a % 2][:], BANK[a % 4][:, 0:TG], ACT.Sigmoid).then_inc(s.ev_act, 1)
                a += 1
        assert a == A_STRAIGHT
        for w in range(6, N_GLU + N_OUT + 2):
            split_hi(N_IN + w, FIRST_GLU + w)
        W1 = N_IN + N_GLU + N_OUT
        for t in range(1, TT + LAG + 1):
            u = t - 1
            if u < TT:
                act.wait_ge(s.acc, B_STRAIGHT - 18 + 2 * (u + 1))
                stats(u, ACC[:, u, :], SQ1[:], TT)
            if LAG <= t < TT + LAG:
                affine(t - LAG, HT1, 2, TT)
            if t > LAG:
                round_hi(t - LAG - 1, HT1, TT)

        def w_hi_loop(ch, i, ahead):
            w, n = W1 + i + 4 * ahead, FIRST_MLP + i + 4 * ahead
            act.wait_ge(raw_in[n % 4], ch * 16 + 16 * (n // 4 + 1))
            if i >= 2:
                act.wait_ge(s.mm_dve, ch * 18 + B_STRAIGHT)
            else:
                act.wait_ge(s.mm_act, ch * 6 + (A_STRAIGHT + 6))
            S.activation(WH[w_slot(w)][:], RAW[n % 4][:], ACT.Copy).then_inc(s.w_hi, 1)

        def act_chunk(ch, last=False):
            for i in range(6):
                if i in (2, 3):
                    w_hi_loop(ch, i, 0)
                act.wait_ge(s.mm_act, ch * 6 + (A_STRAIGHT + i + 1))
                if i >= 2:
                    act.wait_ge(s.f_ready, ch * 6 + (i - 1))
                S.activation(RL[i % 2][:], BANK[i % 4][:, 0:TG], ACT.Relu).then_inc(s.ev_act, 1)
            if not last:
                for i in range(2):
                    w_hi_loop(ch, i, 1)

        with act.Fori(0, NFC - 1) as ch:
            act_chunk(ch)
        act_chunk(NFC - 1, last=True)
        for t in range(TT):
            act.wait_ge(s.acc, B_STRAIGHT + 18 * (NFC - 1) + 2 * (t + 1))
            if t:
                act.wait_ge(s.sq, 2 * TT + t)
            stats(t, ACC[:, t, :], SQ[:], 2 * TT)

    @block.vector
    def _(dve):
        count = [0]

        def then(ins):
            count[0] += 1
            ins.then_inc(s.dve, 1)
            dve.wait_ge(s.dve, count[0])

        tt, ts, stt = V.tensor_tensor, V.tensor_scalar, V.scalar_tensor_tensor
        then(V.memset(PR[:, 0, :], 1.0))
        V.memset(PI[:, 0, :], 0.0).then_inc(s.tabs, 1)
        V.memset(EPSB[:], EPS).then_inc(s.tabs, 1)
        then(V.memset(CSG[0:N, :], 1.0))
        then(V.memset(CSG[N:P, :], -1.0))
        dve.wait_ge(s.pe_small, 1)
        V.tensor_copy(COL[:], BANK[7][:, 0:36]).then_inc(s.col_ready, 1)
        dve.wait_ge(s.tab_dt, 1)
        then(ts(M1[:], AR[:], DT[:], None, ALU.mult))
        then(ts(TH[:], AI[:], DT[:], None, ALU.mult))
        then(ts(KT[:], TH[:], 0.15915494309189535, MAGIC, ALU.mult, ALU.add))
        V.tensor_scalar(KT[:], KT[:], MAGIC, None, ALU.subtract).then_inc(s.tab_th, 1)
        dve.wait_ge(s.tab_th, 1)
        then(stt(RT[:], KT[:], -TWO_PI[0], TH[:], ALU.mult, ALU.add))
        then(stt(RT[:], KT[:], -TWO_PI[1], RT[:], ALU.mult, ALU.add))
        then(stt(RT[:], KT[:], -TWO_PI[2], RT[:], ALU.mult, ALU.add))
        ts(RT[:], RT[:], 3.1415925, -3.1415925, ALU.min, ALU.max).then_inc(s.tab_th, 1)
        dve.wait_ge(s.tab_sin, 2)
        then(tt(C0[:], SH[:], SH[:], ALU.mult))
        then(ts(C0[:], C0[:], -2.0, 1.0, ALU.mult, ALU.add))
        dve.wait_ge(s.tab_e, 1)
        then(tt(TAB[:, 0, 0:N], EX[:], C0[:], ALU.mult))
        then(tt(TAB[:, 1, 0:N], EX[:], SR[:], ALU.mult))
        then(ts(NR[:], TAB[:, 0, 0:N], 1.0, None, ALU.subtract))
        then(tt(M1[:], AR[:], AR[:], ALU.mult))
        then(tt(M2[:], AI[:], AI[:], ALU.mult))
        then(tt(DEN[:], M1[:], M2[:], ALU.add))
        then(V.reciprocal(RD[:], DEN[:]))
        then(tt(M1[:], NR[:], AR[:], ALU.mult))
        then(tt(M2[:], TAB[:, 1, 0:N], AI[:], ALU.mult))
        then(tt(M3[:], TAB[:, 1, 0:N], AR[:], ALU.mult))
        then(tt(M4[:], NR[:], AI[:], ALU.mult))
        then(tt(M1[:], M1[:], M2[:], ALU.add))
        then(tt(M3[:], M3[:], M4[:], ALU.subtract))
        then(tt(TAB[:, 2, 0:N], M1[:], RD[:], ALU.mult))
        then(tt(TAB[:, 3, 0:N], M3[:], RD[:], ALU.mult))
        V.tensor_copy(TAB[:, :, N:P], TAB[:, :, 0:N]).then_inc(s.tabs, 1)
        def to_state(d, j0):
            q0 = d * G
            for j in range(j0, j0 + 4):
                e = L - 1 - j if d == 0 else j
                out = WB[:, q0:q0 + G, j * SP:(j + 1) * SP]
                pr = PR[:, e, q0:q0 + G].unsqueeze(2).to_broadcast([P, G, SP])
                pi = PI[:, e, q0:q0 + G].unsqueeze(2).to_broadcast([P, G, SP])
                tt(out, B1[:, q0:q0 + G, :], pr, ALU.mult).then_inc(s.dve, 1)
                tt(TW[j % 2][:], B2[:, q0:q0 + G, :], pi, ALU.mult).then_inc(s.dve, 1)
                count[0] += 2
                dve.wait_ge(s.dve, count[0])
                tt(out, out, TW[j % 2][:], ALU.add).then_inc(s.wbt, 1)
                dve.wait_ge(s.wbt, d * L + j + 1)

        def normed(t, src, dst, base):
            dve.wait_ge(s.root, base + t + 1)
            then(V.reciprocal(STAT[2][:, t:t + 1], STAT[1][:, t:t + 1]))
            ts(dst, src, STAT[2][:, t:t + 1], None, ALU.mult).then_inc(s.xn, 1)

        def affine(t, ht, ada, base):
            cond = 0 if t < L else 1
            dve.wait_ge(s.tr, base + t + 1)
            if base + t >= 2:
                dve.wait_ge(s.h_lo, base + t - 1)
            for k in range(4):
                ts(ht[t % 2][:, k, :], turn_banks(t, 6 if base else 2)[0][:, k * P:(k + 1) * P], ADA[ada][:, cond, k:k + 1],
                   ADA[ada + 1][:, cond, k:k + 1], ALU.mult, ALU.add).then_inc(s.aff_d, 1)

        def round_lo(t, ht, base):
            dve.wait_ge(s.h_hi, base + t + 1)
            tt(XL[:, :, t * P:(t + 1) * P], ht[t % 2][:], XH[:, :, t * P:(t + 1) * P].bitcast(F32), ALU.subtract).then_inc(s.h_lo, 1)

        def split_lo(w, n):
            dve.wait_ge(s.w_hi, w + 1)
            tt(WL[w_slot(w)][:], RAW[n % 4][:], WH[w_slot(w)][:].bitcast(F32), ALU.subtract).then_inc(s.w_split, 1)

        def ada_scale(dst, cols, norm, hf):
            for cond in range(2):
                then(stt(dst[:, cond, 4 * hf:4 * hf + 4], cols[:, cond, :], 1.0,
                         COL[:, norm + 4 * hf:norm + 4 * hf + 4], ALU.add, ALU.mult))

        dve.wait_ge(s.pe_small, 2)
        tb = BANK[6][:, 0:4 * Q].rearrange("p (i q) -> p i q", i=4)
        then(V.tensor_copy(PR[:, 1, :], tb[:, 0, :]))
        then(V.tensor_copy(PI[:, 1, :], tb[:, 1, :]))
        then(V.tensor_copy(ZR[:], tb[:, 2, :]))
        then(V.tensor_copy(ZI[:], tb[:, 3, :]))
        dve.wait_ge(s.sgn_ready, 2)
        then(ts(ZS[:], ZI[:], SGN[:], None, ALU.mult))
        then(ts(ZT[:], ZR[:], SGN[:], None, ALU.mult))
        then(ts(ZU[:], ZI[:], -1.0, None, ALU.mult))
        for n in (1, 2, 4):
            br = PR[:, n, :].unsqueeze(1).to_broadcast([P, n, Q])
            bi = PI[:, n, :].unsqueeze(1).to_broadcast([P, n, Q])
            lo, hi = slice(1, n + 1), slice(n + 1, 2 * n + 1)
            then(tt(PR[:, hi, :], PR[:, lo, :], br, ALU.mult))
            then(tt(PT[0][:, 0:n, :], PI[:, lo, :], bi, ALU.mult))
            then(tt(PI[:, hi, :], PR[:, lo, :], bi, ALU.mult))
            then(tt(PT[1][:, 0:n, :], PI[:, lo, :], br, ALU.mult))
            then(tt(PR[:, hi, :], PR[:, hi, :], PT[0][:, 0:n, :], ALU.subtract))
            then(tt(PI[:, hi, :], PI[:, hi, :], PT[1][:, 0:n, :], ALU.add))
        dve.wait_ge(s.b_in, 64)

        def zq(z):
            return z[:].unsqueeze(2).to_broadcast([P, Q, SP])

        then(tt(B1[:], BX[:], zq(ZR), ALU.mult))
        then(tt(TB[:], BY[:], zq(ZS), ALU.mult))
        then(tt(B1[:], B1[:], TB[:], ALU.add))
        then(tt(B2[:], BY[:], zq(ZT), ALU.mult))
        then(tt(TB[:], BX[:], zq(ZU), ALU.mult))
        tt(B2[:], B2[:], TB[:], ALU.add).then_inc(s.tabs, 1)
        dve.wait_ge(s.tabs, 4)

        for t in range(TT):
            normed(t, XS[t][:], XS[t][:], 0)
        dve.wait_ge(s.ada_cols, 4)
        for k in range(4):
            cols = BANK[7][:, 64 + 8 * k:72 + 8 * k].rearrange("p (k a) -> p a k", a=2)
            if k < 2:
                ada_scale(ADA[0], cols, 16, k)
            else:
                V.tensor_copy(ADA[1][:, :, 4 * (k - 2):4 * (k - 2) + 4], cols).then_inc(s.ada0, 1)
        dve.wait_ge(s.ada0, 2)
        affine(0, HT0, 0, 0)
        for t in range(TT):
            if t + 1 < TT:
                affine(t + 1, HT0, 0, 0)
            round_lo(t, HT0, 0)
            if t < 2:
                split_lo(t, FIRST_IN + t)
        for w in range(2, N_IN):
            if w < 6:
                to_state((w - 2) // 2, w % 2 * 4)
            split_lo(w, FIRST_IN + w)
            if w == 5:
                pool_window(dve, tt, then, V.tensor_copy, 0)
                pool_window(dve, tt, then, V.tensor_copy, 1)
            elif w == 6:
                dve.wait_ge(s.st_in, 16)
                V.tensor_copy(STR[:], ST[:].rearrange("q n r -> q r n")).then_inc(s.h0_mm, 1)
                pool_window(dve, tt, then, V.tensor_copy, 2)
        pool_window(dve, tt, then, V.tensor_copy, 3)
        then(V.tensor_copy(AQ[0:N, :], PI[0:N, L, :]))
        then(ts(AQ[N:P, :], PI[N:P, L, :], -1.0, None, ALU.mult))
        dve.wait_ge(s.mm_act, IN_END)
        dve.wait_ge(s.pe_small, 3)
        h0 = BANK[6][:, 0:Q]
        for d in range(2):
            V.tensor_copy(H[:, d, :, 0], h0[:, d * G:(d + 1) * G]).then_inc(s.h_init, 1)
        then(tt(A2R[:], PR[:, L, :], PR[:, L, :], ALU.mult))
        then(tt(A2I[:], PI[:, L, :], PI[:, L, :], ALU.mult))
        then(tt(A2R[:], A2R[:], A2I[:], ALU.subtract))
        then(tt(A2I[:], PR[:, L, :], AQ[:], ALU.mult))
        then(ts(A2I[:], A2I[:], 2.0, None, ALU.mult))

        def chunk_step(g0, src, dst):
            gs = slice(g0, g0 + 8)
            n = dst.stop - dst.start
            n = (n + 1) // 2
            s_, d_ = H[:, :, gs, src], H[:, :, gs, dst]
            p_, q_ = TP[:, :, :, 0:n], TQ[:, :, :, 0:n]
            ar = PR[:, L, :].rearrange("p (d g) -> p d g", d=2)[:, :, gs].unsqueeze(3).to_broadcast([P, 2, 8, n])
            ai = AQ[:].rearrange("p (d g) -> p d g", d=2)[:, :, gs].unsqueeze(3).to_broadcast([P, 2, 8, n])
            then(tt(p_, s_, ar, ALU.mult))
            then(tt(q_[0:N], s_[N:P], ai[N:P], ALU.mult))
            then(tt(q_[N:P], s_[0:N], ai[0:N], ALU.mult))
            then(tt(d_, d_, p_, ALU.add))
            return tt(d_, d_, q_, ALU.add)

        then(V.memset(H[:, :, :, CL], 0.0))
        for k in range(4):
            dve.wait_ge(s.ev_act, 24 + 8 * (k + 1))
            then(chunk_step(8 * k, slice(1, CH - 2, 2), slice(2, CH, 2)))
        for d in range(2):
            V.memset(H[:, d, :, CL], 0.0).then_inc(s.h_init, 1)
        dve.wait_ge(s.h_init, 4)
        row = 2 * G * CH
        lat = [bass.AP(H, p0 * row, [[row, n], [0, 1], [CH, Q], [2, CL // 2]]) for p0, n in ((0, P), (0, N), (N, N))]
        both = [bass.AP(H, p0 * row, [[row, n], [CL, 2], [CH, Q], [2, CC // 2]]) for p0, n in ((0, P), (0, N), (N, N))]

        def at_slot(v, i):
            return v[:, :, :, bass.ds(i, 1)] if not isinstance(i, int) else v[:, :, :, i:i + 1]

        def step(v, i, n):
            full, top, bot = v
            if not isinstance(i, int) or i:
                dve.wait_ge(s.sc_h, i)
            ar = A2R[:].unsqueeze(1).to_broadcast([P, n, Q]).unsqueeze(3)
            ai = A2I[:].unsqueeze(1).to_broadcast([P, n, Q]).unsqueeze(3)
            tt(PS_[:, 0:n].unsqueeze(3), at_slot(full, i), ar, ALU.mult).then_inc(s.sc_p, 1)
            tt(QS_[0:N, 0:n].unsqueeze(3), at_slot(bot, i), ai[N:P], ALU.mult).then_inc(s.sc_p, 1)
            tt(QS_[N:P, 0:n].unsqueeze(3), at_slot(top, i), ai[0:N], ALU.mult).then_inc(s.sc_p, 1)
            dst = at_slot(full, i + 1)
            dve.wait_ge(s.sc_p, i * 3 + 1)
            tt(RS_[:, 0:n].unsqueeze(3), PS_[:, 0:n].unsqueeze(3), dst, ALU.add).then_inc(s.sc_r, 1)
            dve.wait_ge(s.sc_p, i * 3 + 3)
            dve.wait_ge(s.sc_r, i + 1)
            tt(dst, RS_[:, 0:n].unsqueeze(3), QS_[:, 0:n].unsqueeze(3), ALU.add).then_inc(s.sc_h, 1)

        for i in range(CC // 2 - 1):
            step(both, i, 2)
        unroll = 14
        rounds = (CL - CC) // 2 // unroll
        with dve.Fori(CC // 2 - 1, CC // 2 - 1 + (rounds - 1) * unroll + 1, unroll) as i:
            for k in range(unroll):
                step(lat, i + k, 1)
        dve.wait_ge(s.sc_h, CL // 2 - 1)
        for k in range(4):
            chunk_step(8 * k, slice(0, CH - 1, 2), slice(1, CH, 2)).then_inc(s.filled, 1)
            dve.wait_ge(s.filled, k + 1)
        end = H[:, :, :, CH - 1]
        ps, qs = (b[:, 0].rearrange("p (d g) -> p d g", d=2) for b in (PS_, QS_))
        fin, arv, aqv = (v.rearrange("p (d g) -> p d g", d=2) for v in (FIN[:], PR[:, L, :], AQ[:]))
        then(tt(ps, end, arv, ALU.mult))
        then(tt(qs[0:N], end[N:P], aqv[N:P], ALU.mult))
        then(tt(qs[N:P], end[0:N], aqv[0:N], ALU.mult))
        then(tt(fin, fin, ps, ALU.add))
        tt(fin, fin, qs, ALU.add).then_inc(s.cx_h, 1)
        dve.wait_ge(s.acts, 4 + 64 + 4)
        for cond in range(2):
            then(stt(ADA[2][:, cond, :], ADA[2][:, cond, :], 1.0, COL[:, 24:32], ALU.add, ALU.mult))
        for w in range(2):
            split_lo(N_IN + w, FIRST_GLU + w)
        dve.wait_ge(s.fin_mm, 1)
        V.tensor_copy(STO[:], BANK[6][0:Q, 0:P].rearrange("q (r n) -> q n r", r=2)).then_inc(s.fin_ready, 1)
        for g in range(NG):
            cols = slice(g * TG, (g + 1) * TG)
            dve.wait_ge(s.mix_hi, g + 1)
            tt(XL[:, 0:4, cols], POOL[:, :, cols], XH[:, 0:4, cols].bitcast(F32), ALU.subtract).then_inc(s.mix_pool, 1)
        for w in range(2, 4):
            split_lo(N_IN + w, FIRST_GLU + w)
        def gate_out(i):
            o_ = i % 18
            if o_ in (2, 8) and i >= 18:
                w = 4 + 2 * (i // 18) + (0 if o_ == 2 else 1)
                split_lo(N_IN + w, FIRST_GLU + w)
            cond = 0 if o_ // 2 < L else 1
            dve.wait_ge(s.mm_dve, i + 1)
            if i >= 3:
                dve.wait_ge(s.acc, i - 2)
            tt(BT3[i % 3][:], BANK[i % 4][:], GB[:, cond, (o_ % 2) * 512:(o_ % 2) * 512 + 512], ALU.mult).then_inc(s.ev_dve, 1)

        dve.wait_ge(s.gb_in, 16)
        for i in range(18):
            gate_out(i)
            if i in (11, 14, 17):
                g = (i - 11) // 3
                dve.wait_ge(s.y_split_hi, g + 1)
                tt(y_split(g)[1], YR[:, :, g * TG:(g + 1) * TG], y_split(g)[0].bitcast(F32), ALU.subtract).then_inc(s.y_split, 1)
        for w in range(4, 6):
            split_lo(N_IN + w, FIRST_GLU + w)
        a = 0
        for g in range(NG):
            cols = slice(g * TG, (g + 1) * TG)
            for m in range(4):
                dve.wait_ge(s.ev_act, Y_END + a + 1)
                if a:
                    dve.wait_ge(s.mix_ready, a)
                tt(SO[:], SZ[a % 2][:], YR[:, m, cols], ALU.mult).then_inc(s.so, 1)
                dve.wait_ge(s.so, a + 1)
                then(V.tensor_copy(XH[:, 4 + m, cols], SO[:]))
                tt(XL[:, 4 + m, cols], SO[:], XH[:, 4 + m, cols].bitcast(F32), ALU.subtract).then_inc(s.mix_ready, 1)
                a += 1
        for i in range(18, B_STRAIGHT - 18):
            gate_out(i)
        W1 = N_IN + N_GLU + N_OUT
        for t in range(TT + LAG + 1):
            if t < TT:
                for n in range(2):
                    gate_out(B_STRAIGHT - 18 + 2 * t + n)
            u = t - 1
            if 0 <= u < TT:
                if u >= 2:
                    dve.wait_ge(s.tr, TT + u - 1)
                normed(u, ACC[:, u, :], XN[u % 2][:], TT)
            if LAG <= t < TT + LAG:
                affine(t - LAG, HT1, 2, TT)
            if t > LAG:
                round_lo(t - LAG - 1, HT1, TT)
        dve.wait_ge(s.h_lo, 2 * TT)
        dve.wait_ge(s.acc, B_STRAIGHT)

        def lo_loop(ch, i, ahead):
            w, n = W1 + i + 4 * ahead, FIRST_MLP + i + 4 * ahead
            dve.wait_ge(s.w_hi, ch * 4 + (w + 1))
            tt(WL[w_slot(w)][:], RAW[n % 4][:], WH[w_slot(w)][:].bitcast(F32), ALU.subtract).then_inc(s.w_split, 1)

        def square(ch, i):
            g, m = i // 2, i % 2
            cols = slice(g * TG, (g + 1) * TG)
            dve.wait_ge(s.ev_act, ch * 6 + (A_STRAIGHT + i + 1))
            dve.wait_ge(s.mm_dve, ch * 18 + (B_STRAIGHT - 18 + 6 * (g + 1)))
            if i >= 2:
                dve.wait_ge(s.f_ready, ch * 6 + (i - 1))
            tt(FT[i % 2][:], RL[i % 2][:], RL[i % 2][:], ALU.mult).then_inc(s.sqr, 1)
            dve.wait_ge(s.sqr, ch * 12 + (2 * i + 1))
            V.tensor_copy(FH[:, m, cols], FT[i % 2][:]).then_inc(s.sqr, 1)
            dve.wait_ge(s.sqr, ch * 12 + (2 * i + 2))
            tt(FL[:, m, cols], FT[i % 2][:], FH[:, m, cols].bitcast(F32), ALU.subtract).then_inc(s.f_ready, 1)

        def gate(ch, i):
            cond = 0 if i // 2 < L else 1
            dve.wait_ge(s.mm_dve, ch * 18 + (B_STRAIGHT + i + 1))
            dve.wait_ge(s.acc, ch * 18 + (B_STRAIGHT + max(i - 3, 0)))
            tt(BT[i % 4][:], BANK[(6 + i) % 4][:], GB[:, cond, (i % 2) * 512:(i % 2) * 512 + 512], ALU.mult).then_inc(s.ev_dve, 1)

        dve.wait_ge(s.gb_in, 32)

        def chunk(ch, last=False):
            for i in range(6):
                square(ch, i)
                if i in (3, 4):
                    lo_loop(ch, i - 1, 0)
            for i in range(18):
                gate(ch, i)
                if not last and i in (2, 6):
                    lo_loop(ch, 0 if i == 2 else 1, 1)
                if last and i >= 5 and i % 2 == 1:
                    final(i // 2 - 2)

        def final(t):
            dve.wait_ge(s.root, 2 * TT + t + 1)
            then(V.reciprocal(STAT[2][:, t:t + 1], STAT[1][:, t:t + 1]))
            stt(ACC[:, t, :], ACC[:, t, :], STAT[2][:, t:t + 1], NO[:], ALU.mult, ALU.mult).then_inc(s.y_final, 1)

        with dve.Fori(0, NFC - 1) as ch:
            chunk(ch)
        dve.wait_ge(s.no_in, 16)
        chunk(NFC - 1, last=True)
        final(TT - 2)
        final(TT - 1)

    @block.tensor
    def _(pe):
        mm = PE.matmul

        def three(out, stat, mov, first, last):
            (sh_, sl), (mh, ml) = stat, mov
            mm(out, sh_, mh, start=first, stop=False)
            mm(out, sh_, ml, start=False, stop=False)
            return mm(out, sl, mh, start=False, stop=last)

        pe.wait_ge(s.vec_in, 80)
        pe.wait_ge(s.id_ready, 1)
        PE.transpose(BANK[7][:, 0:36], VEC[:], ID[0:36, 0:36]).then_inc(s.pe_small, 1)

        def ada_unit(n, banks, k):
            raw_landed(pe, n)
            cv = COL[:, 0:16].rearrange("p (a k) -> p a k", a=2)[:, :, k]
            for hf in range(2):
                last = mm(BANK[banks[hf]][0:2, :], cv, RAW[n % 4][:, hf * 512:hf * 512 + 512], start=(k == 0), stop=False)
            last.then_inc(s.ada_used, 1)

        pe.wait_ge(s.silu_done, 1)
        pe.wait_ge(s.bias0_in, 32)
        pe.wait_ge(s.sgn_ready, 3)
        for part in range(2):
            for k in range(KB):
                ada_unit(part * KB + k, (2 * part, 2 * part + 1), k)
            for hf in range(2):
                last = mm(BANK[2 * part + hf][0:2, :], ONE[:], BIAS0[:, part * D + hf * 512:part * D + hf * 512 + 512],
                          start=False, stop=True)
            last.then_inc(s.ada_mm, 1)
            if part == 0:
                pe.wait_ge(s.tabs, 3)
                for i in range(4):
                    last = PE.transpose(BANK[6][:, i * Q:(i + 1) * Q], TAB[:, i, :], ID[0:Q, 0:Q])
                last.then_inc(s.pe_small, 1)
        for k in range(4):
            pe.wait_ge(s.row_ready, k + 1)
            for i in range(4):
                last = PE.transpose(BANK[7][:, 64 + 8 * k + 2 * i:66 + 8 * k + 2 * i], ROW0[:, i * P:(i + 1) * P], ID[0:2, 0:2])
            last.then_inc(s.ada_cols, 1)

        def turn_tile(t, src, base):
            pe.wait_ge(s.xn, base + t + 1)
            if t >= 2:
                pe.wait_ge(s.aff_d, 4 * (base + t - 1))
                pe.wait_ge(s.aff_a, 4 * (base + t - 1))
            for k in range(KB):
                last = PE.transpose(turn_banks(t, 6 if base else 2)[k // 4][:, (k % 4) * P:(k % 4 + 1) * P], src[:, k * P:(k + 1) * P], ID[:])
            last.then_inc(s.tr, 1)

        for t in range(TT):
            turn_tile(t, XS[t], 0)

        a = 0

        def bank_free(a):
            if a >= 4:
                pe.wait_ge(s.ev_act, a - 3)
            else:
                pe.wait_ge(s.row_ready, a + 1)

        for mb in range(KB):
            pe.wait_ge(s.w_split, mb + 1)
            wh = WH[mb % 2][:].rearrange("p (k f) -> p k f", k=KB)
            wl = WL[mb % 2][:].rearrange("p (k f) -> p k f", k=KB)
            for g in range(NG):
                if mb == 0:
                    pe.wait_ge(s.h_lo, 3 * (g + 1))
                bank_free(a)
                for k in range(KB):
                    last = three(BANK[a % 4][:, 0:TG], (wh[:, k], wl[:, k]),
                                 (XH[:, k, g * TG:(g + 1) * TG], XL[:, k, g * TG:(g + 1) * TG]), k == 0, k == KB - 1)
                last.then_inc(s.mm_act, 1)
                a += 1
            if mb == 4:
                pe.wait_ge(s.wbt, 16)
                for b in range(16):
                    if b >= 2:
                        pe.wait_ge(s.wb_ready, b - 1)
                    for i in range(4):
                        last = PE.transpose(BANK[6 + b % 2][:, i * P:(i + 1) * P], WB[:, 4 * b + i, :], ID[:])
                    last.then_inc(s.wbt_mm, 1)
        for b in range(32):
            g0, d = 2 * (b // 2), b % 2
            if b == 0:
                pe.wait_ge(s.wb_ready, 16)
                pe.wait_ge(s.u_in0, 16 * 16)
            if b == 16:
                pe.wait_ge(s.u_in1, 16 * 16)
            bank_free(a)
            for i in range(2):
                last = mm(BANK[a % 4][:, i * CH:(i + 1) * CH], WB[:, d * G + g0 + i, :], U[:, g0 + i, :], start=True, stop=True)
            last.then_inc(s.mm_act, 1)
            a += 1
            if b == 3:
                pe.wait_ge(s.h0_mm, 1)
                PE.transpose(BANK[6][:, 0:Q], STR[:].rearrange("q r n -> q (r n)"), ID[0:Q, 0:Q]).then_inc(s.pe_small, 1)
        for b in range(8):
            if b == 0:
                pe.wait_ge(s.cs_in, 48)
                pe.wait_ge(s.h_init, 2)
            if b >= 2:
                pe.wait_ge(s.c_ready, 2 * (b - 1))
            PE.transpose(BANK[6 + b % 2][:, 0:P], CS[:, b, 0:2, :].rearrange("p k n -> p (k n)"), ID[:])
            PE.transpose(BANK[6 + b % 2][:, P:2 * P], CS[:, b, 1:3, :].rearrange("p k n -> p (k n)"), ID[:]).then_inc(s.c_mm, 1)
        def ada_part(part):
            for k in range(KB):
                n = FIRST_ADA2 + part * KB + k
                raw_landed(pe, n)
                if k == 0:
                    if part:
                        pe.wait_ge(s.row_ready, 4 + 2 * part)
                    else:
                        pe.wait_ge(s.aff_a, 4 * TT)
                        pe.wait_ge(s.aff_d, 4 * TT)
                cv = COL[:, 0:16].rearrange("p (a k) -> p a k", a=2)[:, :, k]
                for hf in range(2):
                    last = mm(BANK[4 + hf][0:2, :], cv, RAW[n % 4][:, hf * 512:hf * 512 + 512], start=(k == 0), stop=False)
                last.then_inc(s.ada_used, 1)
            for hf in range(2):
                pe.wait_ge(s.bias_odd_in if hf else s.bias_even_in, 16 * (part + 1))
                mm(BANK[4 + hf][0:2, :], ONE[:], bias_row(2 * part + hf)[:], start=False, stop=True).then_inc(s.ada_mm, 1)
                if part in (1, 2):
                    k_ = 2 * part + hf
                    pe.wait_ge(s.row_ready, 5 + k_)
                    if k_ == 2:
                        pe.wait_ge(s.c_ready, 16)
                    else:
                        pe.wait_ge(s.acts, 68 + k_ - 2)
                    for i in range(4):
                        o = 64 + 8 * (k_ % 4) + 2 * i
                        last = PE.transpose(BANK[7][:, o:o + 2], ROW2[:, i * P:(i + 1) * P], ID[0:2, 0:2])
                    last.then_inc(s.ada_cols, 1)
        for part in range(3):
            ada_part(part)
        pe.wait_ge(s.ca_ready, 16)
        pe.wait_ge(s.dd_ready, 1)
        for b in range(16):
            if b >= 2:
                pe.wait_ge(s.kk_ready, b - 1)
            else:
                pe.wait_ge(s.acts, 72)
            for i in range(2):
                g = 2 * b + i
                o = BANK[6 + b % 2][0:SP, i * 240:(i + 1) * 240]
                mm(o[:, 0:112], B1[:, G + g, :], CA[:, G + g, SP:P], start=(i == 0), stop=False, skip_group_check=True)
                mm(o[:, 112:128], B1[:, G + g, :], C1[:, G + g, :], start=False, stop=False, skip_group_check=True)
                mm(o[:, 112:128], B1[:, g, :], C1[:, g, :], start=False, stop=False, skip_group_check=True)
                mm(o[:, 112:128], ID[0:SP, 0:SP], DD[:, g, :], start=False, stop=True, skip_group_check=True)
                last = mm(o[:, 128:240], B1[:, g, :], CA[:, g, 0:112], start=False, stop=True, skip_group_check=True)
            last.then_inc(s.kk_mm, 1)
        ada_part(3)
        def channel_map(i, a):
            gi, g = i // NG, i % NG
            bank_free(a)
            pe.wait_ge(s.pooled, gi + 1)
            out, src = BANK[a % 4], POOL[:, gi, :]
            lat = src[:, 0:LAT].rearrange("p (c j) -> p j c", j=L)
            if g < 2:
                last = mm(lat_j3(out[:, 0:TG]), PWS[:, gi, :], lat[:, 3 * g:3 * g + 3, :], start=True, stop=True)
            else:
                mm(lat_j3(out[:, 0:256]), PWS[:, gi, :], lat[:, 6:8, :], start=True, stop=True)
                last = mm(out[:, 256:384].rearrange("p (j c) -> p j c", c=CC), PWS[:, gi, :],
                          src[:, LAT:T].rearrange("p (c j) -> p j c", j=L), start=True, stop=True)
            last.then_inc(s.mm_act, 1)

        pe.wait_ge(s.pw_in, 16)
        for i in range(4 * NG):
            channel_map(i, a)
            a += 1
        pe.wait_ge(s.loc_in, 16 * L)
        for b in range(16):
            pe.wait_ge(s.filled, b // 4 + 1)
            bank_free(a)
            for i in range(2):
                g = 2 * b + i
                o = BANK[a % 4][:, i * CH:(i + 1) * CH]
                mm(o, LOC[:, g, :], U[:, g, :], start=True, stop=False, skip_group_check=True)
                mm(o, CA[:, g, :], H[:, 0, g, :], start=False, stop=False, skip_group_check=True)
                mm(o[:, 0:CL], CA[:, G + g, :], H[:, 1, g, CL - 1::-1], start=False, stop=True, skip_group_check=True)
                last = mm(o[:, CL:CH], CA[:, G + g, :], H[:, 1, g, CH - 1:CL - 1:-1], start=False, stop=True,
                          skip_group_check=True)
            last.then_inc(s.mm_act, 1)
            a += 1
        pe.wait_ge(s.cx_h, 1)
        PE.transpose(BANK[6][0:Q, 0:P], FIN[:], ID[:]).then_inc(s.fin_mm, 1)
        def out_pair(b, t):
            for n in range(2):
                o_ = 18 * b + 2 * t + n
                if b == 0:
                    pe.wait_ge(s.mix_pool, t // 3 + 1)
                if b == 2:
                    pe.wait_ge(s.mix_ready, 4 * (t // 3 + 1))
                if o_ < 4:
                    pe.wait_ge(s.ev_act, Y_END - 3 + o_)
                elif 18 <= o_ < 22:
                    pe.wait_ge(s.ev_act, A_STRAIGHT - 3 + o_ % 4)
                else:
                    pe.wait_ge(s.ev_dve, o_ - 3)
                for r in range(2):
                    k, w = 2 * b + r, w_slot(N_IN + (N_GLU + 2 * b if b else 0) + r)
                    last = three(BANK[o_ % 4][:], (XH[:, k, t * P:(t + 1) * P], XL[:, k, t * P:(t + 1) * P]),
                                 (WH[w][:, n * 512:n * 512 + 512], WL[w][:, n * 512:n * 512 + 512]), r == 0, r == 1)
                last.then_inc(s.mm_dve, 1)
        pe.wait_ge(s.w_split, N_IN + 2)
        for t in range(TT):
            out_pair(0, t)
        pe.wait_ge(s.w_split, N_IN + 4)
        for g in range(NG):
            pe.wait_ge(s.y_split, g + 1)
            yh, yl = y_split(g)
            for m in range(4):
                if a < Y_END + 4:
                    pe.wait_ge(s.ev_dve, 15 + (a + 2) % 4)
                else:
                    bank_free(a)
                for k in range(4):
                    wh = WH[w_slot(N_IN + 2 + k // 2)][:].rearrange("p (k f) -> p k f", k=2)[:, k % 2, m * P:(m + 1) * P]
                    wl = WL[w_slot(N_IN + 2 + k // 2)][:].rearrange("p (k f) -> p k f", k=2)[:, k % 2, m * P:(m + 1) * P]
                    last = three(BANK[a % 4][:, 0:TG], (wh, wl), (yh[:, k], yl[:, k]), k == 0, k == 3)
                last.then_inc(s.mm_act, 1)
                a += 1
        for b in range(1, 3):
            pe.wait_ge(s.w_split, N_IN + N_GLU + 2 * b + 2)
            for t in range(TT):
                out_pair(b, t)
        W1 = N_IN + N_GLU + N_OUT

        def hidden(ch, outs):
            for i in outs:
                g, m = i // 2, i % 2
                if i < 4:
                    pe.wait_ge(s.ev_dve, ch * 18 + (B_STRAIGHT - 3 + i))
                else:
                    pe.wait_ge(s.ev_act, ch * 6 + (A_STRAIGHT + i - 3))
                pe.wait_ge(s.h_lo, TT + 3 * (g + 1))
                for k in range(KB):
                    w = w_slot(W1 + k // 4)
                    wh = WH[w][:].rearrange("p (k f) -> p k f", k=4)[:, k % 4, m * P:(m + 1) * P]
                    wl = WL[w][:].rearrange("p (k f) -> p k f", k=4)[:, k % 4, m * P:(m + 1) * P]
                    last = three(BANK[i % 4][:, 0:TG], (wh, wl), (XH[:, k, g * TG:(g + 1) * TG], XL[:, k, g * TG:(g + 1) * TG]),
                                 k == 0, k == KB - 1)
                last.then_inc(s.mm_act, 1)

        def back(ch):
            pe.wait_ge(s.w_split, ch * 4 + (W1 + 4))
            for i in range(18):
                t, n = i // 2, i % 2
                pe.wait_ge(s.f_ready, ch * 6 + 2 * (t // 3 + 1))
                if i < 4:
                    pe.wait_ge(s.ev_act, ch * 6 + (A_STRAIGHT + 3 + i))
                else:
                    pe.wait_ge(s.ev_dve, ch * 18 + (B_STRAIGHT + i - 3))
                for r in range(2):
                    w = w_slot(W1 + 2 + r)
                    last = three(BANK[(6 + i) % 4][:], (FH[:, r, t * P:(t + 1) * P], FL[:, r, t * P:(t + 1) * P]),
                                 (WH[w][:, n * 512:n * 512 + 512], WL[w][:, n * 512:n * 512 + 512]), r == 0, r == 1)
                last.then_inc(s.mm_dve, 1)

        pe.wait_ge(s.w_split, N_IN + N_GLU + N_OUT)
        for t in range(TT):
            out_pair(3, t)
            if t >= LAG - 1:
                turn_tile(t - LAG + 1, XN[(t - LAG + 1) % 2], TT)
        pe.wait_ge(s.w_split, W1 + 2)
        for t in range(TT - LAG + 1, TT):
            hidden(0, [t - (TT - LAG + 1)])
            turn_tile(t, XN[t % 2], TT)
        hidden(0, range(LAG - 1, 6))
        back(0)
        with pe.Fori(1, NFC) as ch:
            pe.wait_ge(s.w_split, ch * 4 + (W1 + 2))
            hidden(ch, range(6))
            back(ch)

    block.__exit__(None, None, None)


_INS = ["x_prompt", "x_sample", "state_ssm", "c", "c_ctx", "norm_mix", "norm_mlp", "w_ada", "b_ada", "w_in", "w_out",
        "pool_w", "pool_scale", "ssm_a_re", "ssm_a_im", "ssm_log_dt", "ssm_b_re", "ssm_b_im", "ssm_c_re", "ssm_c_im",
        "ssm_d", "ssm_w_glu", "w_mlp1", "w_mlp2", "norm_out"]
_OUTS = [(1, CTX, D), (1, LAT, D), (1, 1, 2, G, N, 2)]


def _inverse_counts():
    import numpy as np

    def span(n, w):
        t = np.arange(n)
        return np.clip(t + w // 2, 0, n) - np.clip(t - w // 2, 0, n)

    out = np.empty((4, T), np.float32)
    for i in range(4):
        w = 2 << i
        out[i, :LAT] = (1.0 / np.outer(span(ROWS, w), span(GW, w))).ravel()
        out[i, LAT:] = 1.0 / span(CTX, w)
    return out


def kernel(**inputs):
    import numpy as np
    import concourse.bacc as bacc
    from concourse.bass_utils import run_bass_kernel_spmd

    nc = bacc.Bacc("TRN2", target_bir_lowering=False, num_devices=1)
    arrays = {f"in_{n}": np.ascontiguousarray(inputs[n]) for n in _INS}
    arrays["in_inv_count"] = _inverse_counts()
    args = [nc.dram_tensor(n, a.shape, mybir.dt.from_np(a.dtype), kind="ExternalInput").ap() for n, a in arrays.items()]
    outs = [nc.dram_tensor(f"out_{i}", shape, F32, kind="ExternalOutput").ap() for i, shape in enumerate(_OUTS)]
    build(nc, *args, *outs)
    r = run_bass_kernel_spmd(nc, [arrays], core_ids=[0])
    return tuple(r.results[0][f"out_{i}"] for i in range(len(_OUTS)))
```
